# Optimizing a Trainium2 kernel written in Bass

```python
import math
import jax, jax.numpy as jnp
from jax import lax
import numpy as np

D_MODEL = 1024
BATCH = 1
SEQ = 512
DEPTH = 1

D_MIX = D_MODEL
HGRN_HEADS = 4
HGRN_HEAD_DIM = 128
D_HGRN = HGRN_HEADS * HGRN_HEAD_DIM
HGRN_CHUNK = 64
TMLP_GROUPS = 4
TMLP_GROUP_DIM = 128
D_TMLP = TMLP_GROUPS * TMLP_GROUP_DIM
TMLP_CHUNK = 128
D_IN = 4 * D_HGRN + 2 * D_TMLP
N_EXPERT_GROUPS = 4
EXPERTS_PER_GROUP = 8
N_EXPERTS = N_EXPERT_GROUPS * EXPERTS_PER_GROUP
TOP_K_IN_GROUP = 2
D_EXPERT = 256
RMS_EPS = 1e-6
LN_EPS = 1e-5
F_FLOOR = 1e-30

kernel_name = "hybrid_hgrn2_tokenmlp_hmoe"

def rmsnorm(x, gain):
    x32 = x.astype(jnp.float32)
    y = x32 * lax.rsqrt(jnp.mean(x32 * x32, axis=-1, keepdims=True) + RMS_EPS)
    return y.astype(x.dtype) * gain

def hgrn2_mixer(q_raw, f_raw, i_raw, g_raw, lower_bound, g_norm):
    B, T, _ = q_raw.shape
    H, K, C = HGRN_HEADS, HGRN_HEAD_DIM, HGRN_CHUNK
    nC = T // C
    q = jax.nn.silu(q_raw.astype(jnp.float32))
    lb = lower_bound.astype(jnp.float32)
    f = lb + (1.0 - lb) * jax.nn.sigmoid(f_raw.astype(jnp.float32))
    log_f = jnp.log(jnp.maximum(f, F_FLOOR))
    k = 1.0 - f
    v = i_raw.astype(jnp.float32)

    def to_chunks(a):
        return a.reshape(B, nC, C, H, K).transpose(1, 0, 3, 2, 4)

    mask = jnp.tril(jnp.ones((C, C), dtype=bool))[:, :, None]

    def step(S, inp):
        qc, kc, vc, lfc = inp
        b = jnp.cumsum(lfc, axis=2)
        inter = jnp.einsum('bhtk,bhkv->bhtv', qc * jnp.exp(b), S)
        diff = b[:, :, :, None, :] - b[:, :, None, :, :]
        decay = jnp.where(mask, jnp.exp(jnp.where(mask, diff, 0.0)), 0.0)
        attn = jnp.einsum('bhtk,bhsk,bhtsk->bhts', qc, kc, decay)
        o = inter + jnp.einsum('bhts,bhsv->bhtv', attn, vc)
        b_end = b[:, :, -1, :]
        S = jnp.exp(b_end)[..., None] * S + jnp.einsum(
            'bhsk,bhsv->bhkv', kc * jnp.exp(b_end[:, :, None, :] - b), vc)
        return S, o

    S0 = jnp.zeros((B, H, K, K), jnp.float32)
    _, o = lax.scan(step, S0, (to_chunks(q), to_chunks(k), to_chunks(v), to_chunks(log_f)))
    o = o.transpose(1, 0, 3, 2, 4).reshape(B, T, H, K)
    o = rmsnorm(o, g_norm.astype(jnp.float32))
    g = jax.nn.silu(g_raw.astype(jnp.float32)).reshape(B, T, H, K)
    return (o * g).reshape(B, T, D_HGRN).astype(q_raw.dtype)

def token_mlp_mixer(u_raw, v_raw, ln_g, ln_b, w_s, b_s):
    B, T, _ = u_raw.shape
    G, Cg, P = TMLP_GROUPS, TMLP_GROUP_DIM, TMLP_CHUNK
    nC = T // P
    u = jax.nn.gelu(u_raw, approximate=False).reshape(B, nC, P, G, Cg)
    v = jax.nn.gelu(v_raw, approximate=False).reshape(B, nC, P, G, Cg)
    v32 = v.astype(jnp.float32)
    mu = jnp.mean(v32, axis=-1, keepdims=True)
    var = jnp.mean(jnp.square(v32 - mu), axis=-1, keepdims=True)
    vn = ((v32 - mu) * lax.rsqrt(var + LN_EPS)).astype(v.dtype)
    vn = vn * ln_g.reshape(G, Cg) + ln_b.reshape(G, Cg)
    w = jnp.where(jnp.tril(jnp.ones((P, P), dtype=bool))[None], w_s, 0.0)
    mixed = jnp.einsum('gts,bnsgc->bntgc', w, vn) + b_s.T[None, None, :, :, None]
    return (u * mixed).reshape(B, T, D_TMLP)

def hierarchical_moe(h, w_router_group, w_router_expert, w_gate, w_up, w_down):
    B, T, D = h.shape
    hf = h.reshape(B * T, D)
    p_group = jax.nn.softmax(jnp.einsum('nd,dg->ng', hf, w_router_group).astype(jnp.float32), axis=-1)
    g_idx = jnp.argmax(p_group, axis=-1)
    p_sel = jnp.max(p_group, axis=-1)
    e_logits = jnp.einsum('nd,de->ne', hf, w_router_expert).astype(jnp.float32)
    e_logits = e_logits.reshape(-1, N_EXPERT_GROUPS, EXPERTS_PER_GROUP)
    in_group = jnp.take_along_axis(e_logits, g_idx[:, None, None], axis=1)[:, 0, :]
    top_vals, top_idx = lax.top_k(in_group, TOP_K_IN_GROUP)
    w_top = p_sel[:, None] * jax.nn.softmax(top_vals, axis=-1)
    e_idx = g_idx[:, None] * EXPERTS_PER_GROUP + top_idx
    combine = jnp.sum(jax.nn.one_hot(e_idx, N_EXPERTS, dtype=jnp.float32) * w_top[..., None], axis=1)
    combine = combine.astype(h.dtype).reshape(B, T, N_EXPERTS)

    def per_sequence(args):
        hb, cb = args
        hid = jax.nn.silu(jnp.einsum('td,edf->tef', hb, w_gate)) * jnp.einsum('td,edf->tef', hb, w_up)
        return jnp.einsum('tef,efd->td', hid * cb[..., None], w_down)

    return lax.map(per_sequence, (h, combine))

def setup_inputs(seed: int = 0) -> dict:
    key = jax.random.key(seed)
    ks = jax.random.split(key, 20)
    f32 = jnp.float32
    nrm = lambda k, shape, scale: jax.random.normal(k, shape, f32) * scale
    gain = lambda k, shape: 1.0 + 0.05 * jax.random.normal(k, shape, f32)
    P = TMLP_CHUNK
    return {
        "x": jax.random.normal(ks[0], (BATCH, SEQ, D_MODEL), f32),
        "lb_logits": nrm(ks[1], (DEPTH, D_HGRN), 0.5),
        "norm_mix": gain(ks[2], (DEPTH, D_MODEL)),
        "w_in": nrm(ks[3], (DEPTH, D_MODEL, D_IN), D_MODEL ** -0.5),
        "hgrn_norm": gain(ks[4], (DEPTH, HGRN_HEAD_DIM)),
        "tmlp_ln_g": gain(ks[5], (DEPTH, D_TMLP)),
        "tmlp_ln_b": nrm(ks[6], (DEPTH, D_TMLP), 0.02),
        "w_spatial": nrm(ks[7], (DEPTH, TMLP_GROUPS, P, P), 0.5 * P ** -0.5),
        "b_spatial": 1.0 + nrm(ks[8], (DEPTH, TMLP_GROUPS, P), 0.05),
        "w_out": nrm(ks[9], (DEPTH, D_MIX, D_MODEL), D_MIX ** -0.5),
        "norm_ffn": gain(ks[10], (DEPTH, D_MODEL)),
        "w_router_group": nrm(ks[11], (DEPTH, D_MODEL, N_EXPERT_GROUPS), D_MODEL ** -0.5),
        "w_router_expert": nrm(ks[12], (DEPTH, D_MODEL, N_EXPERTS), D_MODEL ** -0.5),
        "w_gate": nrm(ks[13], (DEPTH, N_EXPERTS, D_MODEL, D_EXPERT), D_MODEL ** -0.5),
        "w_up": nrm(ks[14], (DEPTH, N_EXPERTS, D_MODEL, D_EXPERT), D_MODEL ** -0.5),
        "w_down": nrm(ks[15], (DEPTH, N_EXPERTS, D_EXPERT, D_MODEL), D_EXPERT ** -0.5),
        "norm_final": gain(ks[16], (D_MODEL,)),
    }

def reference(x, lb_logits, norm_mix, w_in, hgrn_norm, tmlp_ln_g, tmlp_ln_b, w_spatial, b_spatial,
              w_out, norm_ffn, w_router_group, w_router_expert, w_gate, w_up, w_down, norm_final):
    p = jax.nn.softmax(lb_logits.astype(jnp.float32), axis=0)
    lower_bounds = jnp.cumsum(p, axis=0) - p[0:1]
    splits = [D_HGRN, 2 * D_HGRN, 3 * D_HGRN, 4 * D_HGRN, 4 * D_HGRN + D_TMLP]
    for layer in range(DEPTH):
        h = rmsnorm(x, norm_mix[layer])
        z = jnp.einsum('btd,de->bte', h, w_in[layer])
        q_r, f_r, i_r, g_r, u_r, v_r = jnp.split(z, splits, axis=-1)
        y_hgrn = hgrn2_mixer(q_r, f_r, i_r, g_r, lower_bounds[layer], hgrn_norm[layer])
        y_tmlp = token_mlp_mixer(u_r, v_r, tmlp_ln_g[layer], tmlp_ln_b[layer],
                                 w_spatial[layer], b_spatial[layer])
        y = jnp.concatenate([y_hgrn, y_tmlp], axis=-1)
        x = x + jnp.einsum('bte,ed->btd', y, w_out[layer])
        h = rmsnorm(x, norm_ffn[layer])
        x = x + hierarchical_moe(h, w_router_group[layer], w_router_expert[layer],
                                 w_gate[layer], w_up[layer], w_down[layer])
    return rmsnorm(x, norm_final)


_drawn_inputs = setup_inputs


def setup_inputs(seed=0):
    import zlib

    import numpy as np

    out = dict(_drawn_inputs(seed))
    spreads = {}
    factors = {'tmlp_ln_g': 2.734, 'tmlp_ln_b': 5.56}
    for name, (base, spread) in spreads.items():
        noise = np.random.default_rng([zlib.crc32(name.encode()), seed]).standard_normal(out[name].shape)
        drawn = base * np.exp(spread * noise) if base else spread * noise
        out[name] = __import__('jax').numpy.asarray(drawn.astype(out[name].dtype))
    for name, factor in factors.items():
        out[name] = (out[name] * factor).astype(out[name].dtype)
    return out
```

```python
from contextlib import ExitStack

import concourse.bass as bass
from concourse import mybir

ALU = mybir.AluOpType
ACT = mybir.ActivationFunctionType
AX = mybir.AxisListType.X
F32 = mybir.dt.float32
BF16 = mybir.dt.bfloat16
I32 = mybir.dt.int32
U32 = mybir.dt.uint32

P = 128
RMS_EPS = 1e-6
LN_EPS = 1e-5
F_FLOOR = 1e-30
SLOTS = 64
RANKS = SLOTS
EMPTY = 4096
LOWEST = -3.0e38


def hybrid_trunk(nc, x, norm_mix, w_in, hgrn_norm, ln_g, ln_b, w_spatial, b_spatial, w_out,
                 norm_ffn, w_rg, w_re, w_gate, w_up, w_down, norm_final, out):
    T, D = x.shape
    NT, KD = T // P, D // P
    G = w_spatial.shape[0]
    C = w_spatial.shape[1]
    NG = w_rg.shape[1]
    NE = w_re.shape[1]
    EPG = NE // NG
    F = w_gate.shape[2]
    KF = F // P
    NL = NG + NE
    HALF = D // 2
    PAIRS = NE // 2
    ROUNDS = T // RANKS
    LEVELS = C.bit_length() - 1
    assert G * C == HALF and C == P and F == 2 * P and NT == 4 and SLOTS * 2 == P
    assert w_in.shape[1] == 6 * HALF and PAIRS % 2 == 0

    h2_rows = nc.dram_tensor("h2_rows", (T, D), F32, kind="Internal").ap()
    expert_rows = nc.dram_tensor("expert_rows", (2 * T, D), F32, kind="Internal").ap()

    w_in_v = w_in.rearrange("(p k) e -> p k e", k=KD)
    w_out_v = w_out.rearrange("(p k) e -> p k e", k=KD)

    with ExitStack() as ctx:
        def sb(name, shape, dt=F32):
            return ctx.enter_context(nc.sbuf_tensor(name, shape, dt))

        def sem(name):
            return ctx.enter_context(nc.semaphore(name))

        x_sb = sb("x_sb", [P, NT, D])
        a_hT = sb("a_hT", [P, KD * T])
        a_ring = sb("a_ring", [P, 2, KD * HALF])
        qT = sb("qT", [P, G, T])
        fT = sb("fT", [P, G, T])
        kT = sb("kT", [P, G, T])
        a_iv = sb("a_iv", [P, 2, NT, HALF])
        y_sb = sb("y_sb", [P, NT, D])
        a_ak = sb("a_ak", [P, 2, G, NT, C])
        wgu0 = sb("wgu0", [P, 2, 2, KD * F])
        wd0 = sb("wd0", [P, 2, KF * D])

        hT = a_hT[:, :].rearrange("p (k t) -> p k t", k=KD)
        states = a_hT[:, 0:G * (NT - 1) * C].rearrange("p (h c v) -> p h c v", h=G, c=NT - 1)
        squares = a_hT[:, 2048:2048 + 2 * HALF].rearrange("p (b n) -> p b n", b=2)
        junk = a_ak[:, :, :, :, :].rearrange("p a h c v -> p (a h c v)").rearrange("p (t d) -> p t d", t=NT)
        junk_last = a_ring[:, 0, :].rearrange("p (t d) -> p t d", t=NT)
        i_tok, v_tok = a_iv[:, 0], a_iv[:, 1]
        h2 = a_iv[:, :, :, :].rearrange("p a t n -> p (a t n)").rearrange("p (t d) -> p t d", t=NT)
        attn, k_tok = a_ak[:, 0], a_ak[:, 1]
        wgu = [wgu0[:, :, :, :], a_ring[:, :, :].rearrange("p e (g n) -> p e g n", g=2)]
        wd = [wd0[:, :, :], a_hT[:, :].rearrange("p (e n) -> p e n", e=2)]
        hg = [qT[:, :, :].rearrange("p h t -> p (h t)")[:, b * D:(b + 1) * D] for b in range(2)]
        fT_flat = fT[:, :, :].rearrange("p h t -> p (h t)")
        hgT = fT_flat[:, 0:KD * P].rearrange("p (k s) -> p k s", k=KD)
        silu_g = fT_flat[:, KD * P:KD * P + F]
        hid = fT_flat[:, KD * P + F:KD * P + 2 * F]
        hidT = fT_flat[:, KD * P + 2 * F:KD * P + 3 * F].rearrange("p (k s) -> p k s", k=KF)
        yo = [kT[:, :, :].rearrange("p h t -> p (h t)")[:, b * D:(b + 1) * D] for b in range(2)]
        er = [a_iv[:, b].rearrange("p t n -> p (t n)").rearrange("p (j d) -> p j d", j=2) for b in range(2)]

        ident = sb("ident", [P, P])
        ones_b = sb("ones_b", [P, P], BF16)
        before_b = sb("before_b", [P, P], BF16)
        level_mask = sb("level_mask", [P, LEVELS, C])
        gain_mix = sb("gain_mix", [P, KD])
        gnorm = sb("gnorm", [P, C])
        lng = sb("lng", [P, HALF])
        lnb = sb("lnb", [P, HALF])
        ws_raw = sb("ws_raw", [P, G, C])
        wsT = sb("wsT", [P, G, C])
        bs_raw = sb("bs_raw", [G, C])
        bsT = sb("bsT", [P, G])
        gain_ffn = sb("gain_ffn", [P, D])
        wr_g = sb("wr_g", [P, KD, NG])
        wr_e = sb("wr_e", [P, KD, NE])
        wr = sb("wr", [P, KD, NL])
        stat_x, stat_2, stat_f = (sb(n, [P, NT, 4]) for n in ("stat_x", "stat_2", "stat_f"))
        bn6 = sb("bn6", [P, NT, G, 6])
        bn2 = sb("bn2", [P, NT * G, 2])
        ln_r = sb("ln_r", [P, NT * G])
        o_ss = sb("o_ss", [P, G, NT])
        o_r = sb("o_r", [P, G, NT])
        tab = sb("tab", [P, 2, ROUNDS * PAIRS], I32)
        cur = sb("cur", [P, 4], I32)
        steps = sb("steps", [P, 1], I32)
        w_top = sb("w_top", [P, 2, NT])

        rt_flat = a_ak[:, :, :, :, :].rearrange("p a h c v -> p (a h c v)")
        rt_used = [0]

        def rt(*shape):
            n = 1
            for s in shape:
                n *= s
            v = rt_flat[:, rt_used[0]:rt_used[0] + n]
            rt_used[0] += n
            assert rt_used[0] <= 2 * G * NT * C
            if len(shape) == 2:
                return v.rearrange("p (a b) -> p a b", a=shape[0])
            if len(shape) == 3:
                return v.rearrange("p (a b c) -> p a b c", a=shape[0], b=shape[1])
            if len(shape) == 4:
                return v.rearrange("p (a b c d) -> p a b c d", a=shape[0], b=shape[1], c=shape[2])
            return v

        logits = rt(NT, NL)
        g_max = rt(NT, 1)
        g_exp = rt(NT, NG)
        g_sum = rt(NT)
        p_sel = rt(NT)
        g_pick = rt(NT, NG)
        g_hot = rt(NT, NG)
        e_log = rt(NT, NE)
        top8 = rt(NT, 8)
        idx8 = rt(NT, 8)
        top_i = rt(NT, 2)
        gap = rt(NT)
        egap = rt(NT)
        den = rt(NT)
        hot = rt(NT, 2, NE)
        rank_all = rt(NT, 2, NE)
        rank = rt(NT * 2)
        round_rank = rt(NT * 2)
        deal = rt(NT * 2, 2, 2, PAIRS)
        in_round = rt(2, NT * 2, SLOTS)
        most = rt(1)
        over = rt(ROUNDS)
        gain_fin = rt(D)
        hot_b = sb("hot_b", [P, NT, NE], BF16)
        iota_e = sb("iota_e", [P, NE])
        iota_s = sb("iota_s", [P, SLOTS])
        iota_i = sb("iota_i", [P, SLOTS], I32)
        row_i = sb("row_i", [P, 2, NT, 2], I32)
        row_f = sb("row_f", [P, 2, NT, 2])
        first_w = sb("first_w", [P, NG])
        limits = sb("limits", [P, ROUNDS])

        bank = ctx.enter_context(nc.psum_tensor("bank", [P, 8, HALF], F32))

        s_x = [sem(f"x_loaded{t}") for t in range(NT)]
        s_small = sem("small_loaded")
        s_ring = [sem(f"ring_loaded{b}") for b in range(2)]
        s_const = sem("const_made")
        s_cstep = sem("const_step")
        x_ss = sem("x_ss")
        x_ms = sem("x_ms")
        x_sd = sem("x_sd")
        xn_ready = sem("xn_ready")
        xT_done = sem("xT_done")
        hT_even = sem("hT_even")
        hT_odd = sem("hT_odd")
        wsT_done = sem("wsT_done")
        wsT_ready = sem("wsT_ready")
        z_done = sem("z_done")
        z_out = sem("z_out")
        fk_ready = sem("fk_ready")
        attn_done = sem("attn_done")
        attn_kept = sem("attn_kept")
        decayed = sem("decayed")
        f_merged = sem("f_merged")
        bn_done = sem("bn_done")
        ln_sd = sem("ln_sd")
        ln_norm = sem("ln_norm")
        vn_ready = sem("vn_ready")
        gg_ready = sem("gg_ready")
        mixed_done = sem("mixed_done")
        u_ready = sem("u_ready")
        kt_done = sem("ktok_done")
        kt_ready = sem("ktok_ready")
        upd_done = sem("update_done")
        state_ready = sem("state_ready")
        o_done = sem("o_done")
        o_sq = sem("o_sq")
        o_ms = sem("o_ms")
        o_sd = sem("o_sd")
        y_ready = sem("y_ready")
        yT_done = sem("yT_done")
        yT_a = sem("yT_act")
        yT_d = sem("yT_dve")
        wo_done = sem("w_out_done")
        x2_ready = sem("x2_ready")
        x2_ss = sem("x2_ss")
        x2_ms = sem("x2_ms")
        x2_sd = sem("x2_sd")
        h2_ready = sem("h2_ready")
        h2_stored = sem("h2_stored")
        h2T_done = sem("h2T_done")
        h2T_a = sem("h2T_act")
        h2T_d = sem("h2T_dve")
        logit_done = sem("logits_done")
        r_dve = sem("router_dve")
        r_act = sem("router_act")
        rank_ops = sem("rank_ops")
        rank_done = sem("rank_done")
        steps_ready = sem("steps_ready")
        deal_ready = sem("deal_ready")
        round_ready = sem("round_ready")
        slots_done = sem("slots_done")
        tab_ready = sem("tab_ready")
        hg_clear = sem("hg_clear")
        wgu_loaded = [sem(f"wgu_loaded{b}") for b in range(2)]
        wd_loaded = [sem(f"wd_loaded{b}") for b in range(2)]
        cur_ready = sem("cur_ready")
        gathered = [sem(f"gathered{b}") for b in range(2)]
        scattered = [sem(f"scattered{b}") for b in range(2)]
        hgT_done = sem("hgT_done")
        hgT_a = sem("hgT_act")
        hgT_d = sem("hgT_dve")
        gu_done = sem("gate_up_done")
        silu_done = sem("silu_done")
        hid_ready = sem("hid_ready")
        hidT_done = sem("hidT_done")
        hidT_ready = sem("hidT_ready")
        down_done = sem("down_done")
        yo_a = sem("yo_act")
        yo_d = sem("yo_dve")
        er_loaded = [sem(f"er_loaded{b}") for b in range(2)]
        fin_loaded = sem("gain_fin_loaded")
        f_dve = sem("final_dve")
        f_y = sem("final_y")
        f_ss = sem("final_ss")
        f_ms = sem("final_ms")
        f_sd = sem("final_sd")
        f_out = sem("final_out")
        out_stored = sem("out_stored")
        s_dve = sem("dve_step")

        block = ctx.enter_context(nc.Block())

        SMALL = 9
        BLOCKS = 8
        NZ = 6 * NT
        COL = [1, 0, 5, 2, 3, 4]
        LEVEL_AT = [2 * NT + 2 * n for n in range(LEVELS + 1)]
        Z_BANKS = 3

        def double_steps(eng):
            extra = eng.value_load(steps[0:1, 0:1], min_val=0, max_val=(ROUNDS - 1) * PAIRS // 2)
            return extra + PAIRS // 2

        def pair_w(w, q):
            return w[q * 2:q * 2 + 2] if isinstance(q, int) else w[bass.ds(q * 2, 2)]

        def load_gate_up(sp, b, q):
            for g, w in enumerate((w_gate, w_up)):
                sp.dma_start(wgu[b][:, :, g, :],
                             pair_w(w, q).rearrange("e (p k) f -> p e (k f)", k=KD)).then_inc(wgu_loaded[b], 16)

        def load_down(sp, b, q):
            sp.dma_start(wd[b], pair_w(w_down, q).rearrange("e (p k) d -> p e (k d)", k=KF))\
              .then_inc(wd_loaded[b], 16)

        @block.sync
        def _(sp):
            for t in range(NT):
                sp.dma_start(x_sb[:, t, :], x[t * P:(t + 1) * P, :]).then_inc(s_x[t], 16)
            for j in range(BLOCKS):
                src = w_in_v[:, :, COL[j] * HALF:(COL[j] + 1) * HALF] if j < 6 \
                    else w_out_v[:, :, (j - 6) * HALF:(j - 5) * HALF]
                if j >= 2:
                    sp.wait_ge(z_done, NT * (j - 1))
                sp.dma_start(a_ring[:, j % 2, :].rearrange("p (k n) -> p k n", k=KD), src)\
                  .then_inc(s_ring[j % 2], 16)
                if j == 1:
                    load_gate_up(sp, 0, 0)
                    load_down(sp, 0, 0)
            for t in range(NT):
                sp.wait_ge(h2_ready, t + 1)
                sp.dma_start(h2_rows[t * P:(t + 1) * P, :], h2[:, t, :]).then_inc(h2_stored, 16)
            sp.wait_ge(wo_done, 2 * NT)
            load_gate_up(sp, 1, 1)
            sp.wait_ge(logit_done, NT)
            load_down(sp, 1, 1)
            sp.wait_ge(steps_ready, 1)
            n_double = double_steps(sp)
            with sp.Fori(1, n_double) as m:
                for b in range(2):
                    q = (m % (PAIRS // 2)) * 2 + b
                    sp.wait_ge(gu_done, m * 2 + (b - 1))
                    load_gate_up(sp, b, q)
                    sp.wait_ge(down_done, m * 2 + (b - 1))
                    load_down(sp, b, q)
            for b in range(2):
                sp.wait_ge(scattered[b], n_double * 16)
            for t in range(NT):
                if t >= 2:
                    sp.wait_ge(f_y, t - 1)
                sp.dma_start(er[t % 2], expert_rows[2 * t * P:2 * (t + 1) * P, :]
                             .rearrange("(p j) d -> p j d", j=2)).then_inc(er_loaded[t % 2], 16)
            for t in range(NT):
                sp.wait_ge(f_out, t + 1)
                sp.dma_start(out[t * P:(t + 1) * P, :], y_sb[:, t, :]).then_inc(out_stored, 16)
            sp.wait_ge(out_stored, 16 * NT)

        @block.gpsimd
        def _(pool):
            made = [0]

            def step(ins):
                made[0] += 1
                ins.then_inc(s_cstep, 1)
                pool.wait_ge(s_cstep, made[0])

            step(pool.memset(ident[:, :], 0.0))
            pool.affine_select(out=ident[:, :], in_=ident[:, :], compare_op=ALU.not_equal, fill=1.0, base=0,
                               pattern=[[-1, P]], channel_multiplier=1).then_inc(s_const, 1)
            pool.wait_ge(s_small, 16 * SMALL)
            pool.affine_select(out=ws_raw[:, :, :], in_=ws_raw[:, :, :], compare_op=ALU.is_ge, fill=0.0, base=0,
                               pattern=[[0, G], [-1, C]], channel_multiplier=1).then_inc(s_const, 1)
            step(pool.memset(level_mask[:, :, :], 0.0))
            for n in range(LEVELS):
                h = 1 << n
                right = level_mask[:, n, :].rearrange("p (b two j) -> p b two j", two=2, j=h)[:, :, 1, :]
                nb = C // (2 * h)
                step(pool.memset(right, 1.0))
                step(pool.affine_select(out=right, in_=right, compare_op=ALU.is_ge, fill=0.0, base=0,
                                        pattern=[[-2 * h, nb], [0, h]], channel_multiplier=1))
                last = pool.affine_select(out=right, in_=right, compare_op=ALU.is_ge, fill=0.0, base=h - 1,
                                          pattern=[[2 * h, nb], [0, h]], channel_multiplier=-1)
            last.then_inc(s_const, 1)
            step(pool.memset(ones_b[:, :], 1.0))
            pool.affine_select(out=before_b[:, :], in_=ones_b[:, :], compare_op=ALU.is_gt, fill=0.0, base=0,
                               pattern=[[1, P]], channel_multiplier=-1).then_inc(s_const, 1)
            step(pool.iota(iota_i[:, :], pattern=[[1, SLOTS]], base=0, channel_multiplier=0))
            pool.tensor_copy(iota_e[:, :], iota_i[:, 0:NE])
            pool.tensor_copy(iota_s[:, :], iota_i[:, :])
            pool.iota(row_i[:, 0], pattern=[[P, NT], [0, 2]], base=-EMPTY, channel_multiplier=1)
            step(pool.iota(row_i[:, 1], pattern=[[2 * P, NT], [1, 2]], base=-EMPTY, channel_multiplier=2))
            pool.tensor_copy(row_f[:, :, :, :], row_i[:, :, :, :])
            pool.tensor_scalar(first_w[:, :], iota_i[:, 0:NG], -1.0, float(NG), ALU.mult, ALU.add)
            pool.tensor_scalar(limits[:, :], iota_i[:, 0:ROUNDS], float(RANKS), 0.0, ALU.mult, ALU.add)
            pool.tensor_copy(wr[:, :, 0:NG], wr_g[:, :, :])
            pool.tensor_copy(wr[:, :, NG:NL], wr_e[:, :, :]).then_inc(s_const, 1)
            pool.wait_ge(ln_norm, NT)
            for t in range(NT):
                step(pool.tensor_tensor(v_tok[:, t, :], v_tok[:, t, :], lng[:, :], ALU.mult))
                pool.tensor_tensor(v_tok[:, t, :], v_tok[:, t, :], lnb[:, :], ALU.add).then_inc(vn_ready, 1)
            for t in range(NT):
                pool.wait_ge(z_out, 4 * NT + t + 1)
                gt = y_sb[:, t, 0:HALF].rearrange("p (h v) -> p h v", h=G)
                pool.tensor_tensor(gt, gt, gnorm[:, :].unsqueeze(1).to_broadcast([P, G, C]), ALU.mult)\
                    .then_inc(gg_ready, 1)
            pool.wait_ge(o_done, G)
            for b in range(2):
                pool.memset(hg[b], 0.0).then_inc(hg_clear, 1)

            pool.wait_ge(steps_ready, 1)
            n_double = double_steps(pool)
            pool.wait_ge(h2_stored, 16 * NT)
            pool.wait_ge(hg_clear, 2)

            def pick(kind, b, step_n, n):
                c = 2 * kind + b
                col = step_n if isinstance(step_n, int) else bass.ds(step_n, 1)
                src = tab[:, kind, col:col + 1] if isinstance(step_n, int) else tab[:, kind, col]
                pool.tensor_copy(cur[:, c:c + 1], src).then_inc(cur_ready, 1)
                pool.wait_ge(cur_ready, n)
                return cur[:, c:c + 1]

            def gather(b, step_n, n, limit):
                pool.indirect_dma_start(
                    hg[b], None, h2_rows, bass.IndirectOffsetOnAxis(ap=pick(0, b, step_n, n), axis=0),
                    bounds_check=limit(), oob_is_err=False).then_inc(gathered[b], 16)

            def scatter(b, step_n, n, limit):
                pool.indirect_dma_start(
                    expert_rows, bass.IndirectOffsetOnAxis(ap=pick(1, b, step_n, n), axis=0), yo[b], None,
                    bounds_check=limit(), oob_is_err=False).then_inc(scattered[b], 16)

            pool.wait_ge(tab_ready, 1)
            gather(0, 0, 1, lambda: T - 1)
            gather(1, 1, 2, lambda: T - 1)
            pool.wait_ge(hgT_done, 1)
            gather(0, 2, 3, lambda: T - 1)
            pool.wait_ge(yo_a, 1)
            pool.wait_ge(yo_d, 1)
            scatter(0, 0, 4, lambda: 2 * T - 1)
            pool.wait_ge(hgT_done, 2)
            gather(1, 3, 5, lambda: T - 1)
            pool.wait_ge(tab_ready, ROUNDS)
            with pool.Fori(2, n_double) as m:
                for b in range(2):
                    pool.wait_ge(yo_a, m * 2 + (b - 2))
                    pool.wait_ge(yo_d, m * 2 + (b - 2))
                    scatter(1 - b, m * 2 + (b - 3), m * 4 + (2 * b - 2),
                            lambda: pool.snap(m + (2 * T - 1 + b)))
                    pool.wait_ge(hgT_done, m * 2 + (b - 1))
                    gather(b, m * 2 + b, m * 4 + (2 * b - 1), lambda: pool.snap(m + (T - 1 + 4 * b)))
            for k in range(3):
                b = (k + 1) % 2
                pool.wait_ge(yo_a, n_double * 2 + (k - 2))
                pool.wait_ge(yo_d, n_double * 2 + (k - 2))
                scatter(b, n_double * 2 + (k - 3), n_double * 4 + (k - 2),
                        lambda: pool.snap(n_double + (2 * T - 1 + 8 * k)))

        @block.scalar
        def _(act):
            loads = [(gain_mix[:, :], norm_mix.rearrange("(p k) -> p k", k=KD)),
                     (ws_raw[:, :, :], w_spatial.rearrange("g t s -> t g s")),
                     (bs_raw[:, :], b_spatial),
                     (gnorm[:, :], hgrn_norm.unsqueeze(0).to_broadcast([P, C])),
                     (lng[:, :], ln_g.unsqueeze(0).to_broadcast([P, HALF])),
                     (lnb[:, :], ln_b.unsqueeze(0).to_broadcast([P, HALF])),
                     (gain_ffn[:, :], norm_ffn.unsqueeze(0).to_broadcast([P, D])),
                     (wr_g[:, :, :], w_rg.rearrange("(p k) e -> p k e", k=KD)),
                     (wr_e[:, :, :], w_re.rearrange("(p k) e -> p k e", k=KD))]
            assert len(loads) == SMALL
            for dst, src in loads:
                act.dma_start(dst, src).then_inc(s_small, 16)
            for t in range(NT):
                act.wait_ge(s_x[t], 16)
                act.activation(junk[:, t, :], x_sb[:, t, :], ACT.Square, accum_out=stat_x[:, t, 0:1]).then_inc(x_ss, 1)
            act.wait_ge(x_ms, 1)
            act.activation(stat_x[:, :, 2], stat_x[:, :, 1], ACT.Sqrt).then_inc(x_sd, 1)
            act.wait_ge(s_small, 16 * SMALL)
            for k in range(0, KD, 2):
                act.wait_ge(xT_done, k + 1)
                act.activation(hT[:, k, :], bank[:, 3, :], ACT.Copy, scale=gain_mix[:, k:k + 1])\
                   .then_inc(hT_even, 1)
            act.wait_ge(wsT_done, 1)
            act.activation(wsT[:, :, :].rearrange("p g t -> p (g t)"), bank[:, 5, :], ACT.Copy)
            act.activation(bsT[:, :], bank[:, 6, 0:G], ACT.Copy).then_inc(wsT_ready, 1)
            for j in range(NZ):
                blk, t = divmod(j, NT)
                dst, fn = [(fT[:, t, :], ACT.Sigmoid), (qT[:, t, :], ACT.Silu), (v_tok[:, t, :], ACT.Gelu),
                           (i_tok[:, t, :], ACT.Copy), (y_sb[:, t, 0:HALF], ACT.Silu),
                           (y_sb[:, t, HALF:D], ACT.Gelu)][blk]
                if j == 4 * NT:
                    act.wait_ge(bn_done, 1)
                    act.activation(ln_r[:, :], bn2[:, :, 1], ACT.Sqrt).then_inc(ln_sd, 1)
                act.wait_ge(z_done, j + 1)
                act.activation(dst, bank[:, j % Z_BANKS, :], fn).then_inc(z_out, 1)
            for h in range(G):
                act.wait_ge(kt_done, h + 1)
                act.activation(k_tok[:, h].rearrange("p c k -> p (c k)"), bank[:, 5 + h % 2, :], ACT.Copy)\
                   .then_inc(kt_ready, 1)
            for h in range(G):
                act.wait_ge(o_done, h + 1)
                if h >= 2:
                    act.wait_ge(o_ms, h - 1)
                act.activation(squares[:, h % 2, :], bank[:, [2, 7, 3, 4][h], :], ACT.Square).then_inc(o_sq, 1)
            act.wait_ge(o_ms, G + 1)
            act.activation(o_r[:, :, :], o_ss[:, :, :], ACT.Sqrt).then_inc(o_sd, 1)

            def h2T_out(t):
                act.wait_ge(h2T_done, t + 1)
                act.activation(hT[:, 0:4, t * P:(t + 1) * P], bank[:, 2, :].rearrange("p (k t) -> p k t", k=4),
                               ACT.Copy).then_inc(h2T_a, 1)

            for t in range(NT):
                act.wait_ge(yT_done, t + 1)
                act.activation(hT[:, 0:4, t * P:(t + 1) * P], bank[:, 0, :].rearrange("p (k t) -> p k t", k=4),
                               ACT.Copy).then_inc(yT_a, 1)
                if t >= 1:
                    h2T_out(t - 1)
                act.wait_ge(x2_ready, t + 1)
                act.activation(junk[:, t, :], x_sb[:, t, :], ACT.Square, accum_out=stat_2[:, t, 0:1]).then_inc(x2_ss, 1)
                act.wait_ge(x2_ms, t + 1)
                act.activation(stat_2[:, t, 2:3], stat_2[:, t, 1:2], ACT.Sqrt).then_inc(x2_sd, 1)
            h2T_out(NT - 1)
            act.wait_ge(x2_ss, NT)
            act.dma_start(gain_fin, norm_final.unsqueeze(0).to_broadcast([P, D])).then_inc(fin_loaded, 16)
            act.wait_ge(r_dve, 1)
            act.activation(g_exp, g_exp, ACT.Exp).then_inc(r_act, 1)
            act.wait_ge(r_dve, 2)
            act.activation(egap, gap, ACT.Exp).then_inc(r_act, 1)

            act.wait_ge(steps_ready, 1)
            n_double = double_steps(act)

            def gathered_T(n):
                act.wait_ge(hgT_done, n)
                act.activation(hgT[:, 0:4, :], bank[:, 3, :].rearrange("p (k s) -> p k s", k=4), ACT.Copy)\
                   .then_inc(hgT_a, 1)

            def silu(n):
                act.wait_ge(gu_done, n)
                act.activation(silu_g, bank[:, 0, 0:F], ACT.Silu).then_inc(silu_done, 1)

            def hidden_T(n):
                act.wait_ge(hidT_done, n)
                act.activation(hidT, bank[:, 5, 0:F].rearrange("p (k s) -> p k s", k=KF), ACT.Copy)\
                   .then_inc(hidT_ready, 1)

            def rows_out(b, n, uses):
                act.wait_ge(down_done, n)
                if uses is not None:
                    act.wait_ge(scattered[b], uses)
                act.activation(yo[b][:, 0:HALF], bank[:, 1, :], ACT.Copy).then_inc(yo_a, 1)

            gathered_T(1)
            silu(1)
            gathered_T(2)
            hidden_T(1)
            silu(2)
            rows_out(0, 1, None)
            gathered_T(3)
            hidden_T(2)
            silu(3)
            rows_out(1, 2, None)
            gathered_T(4)
            hidden_T(3)
            with act.Fori(1, n_double - 1) as i:
                for b in (1, 0):
                    o = 1 if b else 2
                    silu(i * 2 + (o + 1))
                    rows_out(1 - b, i * 2 + o, i * 16)
                    gathered_T(i * 2 + (o + 2))
                    hidden_T(i * 2 + (o + 1))
            silu(n_double * 2)
            rows_out(0, n_double * 2 - 1, n_double * 16 - 16)
            hidden_T(n_double * 2)
            rows_out(1, n_double * 2, n_double * 16 - 16)

            for t in range(NT):
                act.wait_ge(f_y, t + 1)
                act.activation(junk_last[:, t, :], x_sb[:, t, :], ACT.Square, accum_out=stat_f[:, t, 0:1])\
                   .then_inc(f_ss, 1)
                act.wait_ge(f_ms, t + 1)
                act.activation(stat_f[:, t, 2:3], stat_f[:, t, 1:2], ACT.Sqrt).then_inc(f_sd, 1)

        @block.vector
        def _(dve):
            n_link = [0]

            def link(ins):
                n_link[0] += 1
                ins.then_inc(s_dve, 1)
                dve.wait_ge(s_dve, n_link[0])

            dve.memset(tab[:, :, :], EMPTY)
            dve.wait_ge(x_ss, NT)
            dve.tensor_scalar(stat_x[:, :, 1], stat_x[:, :, 0], 1.0 / D, RMS_EPS, ALU.mult, ALU.add).then_inc(x_ms, 1)
            dve.wait_ge(x_sd, 1)
            link(dve.reciprocal(stat_x[:, :, 3], stat_x[:, :, 2]))
            for t in range(NT):
                dve.tensor_scalar(y_sb[:, t, :], x_sb[:, t, :], stat_x[:, t, 3:4], None, ALU.mult)\
                   .then_inc(xn_ready, 1)
            dve.wait_ge(s_small, 16 * SMALL)
            for k in range(1, KD, 2):
                dve.wait_ge(xT_done, k + 1)
                dve.tensor_scalar(hT[:, k, :], bank[:, 4, :], gain_mix[:, k:k + 1], None, ALU.mult)\
                   .then_inc(hT_odd, 1)
            for h in range(G):
                dve.wait_ge(z_out, h + 1)
                dve.tensor_scalar(kT[:, h, :], fT[:, h, :], -1.0, 1.0, ALU.mult, ALU.add)
                dve.tensor_scalar(fT[:, h, :], fT[:, h, :], F_FLOOR, None, ALU.max).then_inc(fk_ready, 1)

            def merge(n, h):
                j = 1 << (n - 1)
                f = fT[:, h, :].rearrange("p (b two j) -> p b two j", two=2, j=j)
                dve.wait_ge(decayed, n * G + h + 1)
                dve.tensor_tensor(f[:, :, 1, j - 1], f[:, :, 1, j - 1], f[:, :, 0, j - 1],
                                  ALU.mult).then_inc(f_merged, 1)

            def level(n):
                for h in range(G):
                    u = n * G + h
                    dve.wait_ge(attn_done, u + 1)
                    src = bank[:, 5 + h % 2, :].rearrange("p (c t) -> p c t", c=NT)
                    if n == 0:
                        dve.wait_ge(s_const, 5)
                        dve.tensor_tensor(attn[:, h], src, ident[:, :].unsqueeze(1).to_broadcast([P, NT, C]),
                                          ALU.mult).then_inc(attn_kept, 1)
                        dve.wait_ge(fk_ready, G)
                        dve.tensor_tensor(qT[:, h, :], qT[:, h, :], fT[:, h, :], ALU.mult).then_inc(decayed, 1)
                        continue
                    dve.wait_ge(attn_kept, u - G + 1)
                    dve.copy_predicated(attn[:, h], level_mask[:, n - 1, :].unsqueeze(1).to_broadcast([P, NT, C])
                                        .bitcast(I32), src).then_inc(attn_kept, 1)
                    j = 1 << (n - 1)
                    q, k, f = (a[:, h, :].rearrange("p (b two j) -> p b two j", two=2, j=j) for a in (qT, kT, fT))
                    nb = T // (2 * j)
                    if n >= 2:
                        dve.wait_ge(f_merged, (n - 2) * G + h + 1)
                    dve.wait_ge(decayed, (n - 1) * G + h + 1)
                    dve.tensor_tensor(q[:, :, 1, :], q[:, :, 1, :],
                                      f[:, :, 0, j - 1:j].to_broadcast([P, nb, j]), ALU.mult)
                    dve.tensor_tensor(k[:, :, 0, :], k[:, :, 0, :],
                                      f[:, :, 1, j - 1:j].to_broadcast([P, nb, j]), ALU.mult).then_inc(decayed, 1)
                    if h >= 1:
                        merge(n, h - 1)
                if n >= 1:
                    merge(n, G - 1)

            level(0)
            level(1)
            for t in range(NT):
                dve.wait_ge(z_out, 2 * NT + t + 1)
                for g in range(G):
                    last = dve.bn_stats(bn6[:, t, g, :], v_tok[:, t, g * C:(g + 1) * C])
                link(last)
                for g in range(G):
                    last = dve.bn_aggr(bn2[:, t * G + g, :], bn6[:, t, g, :])
            link(last)
            dve.tensor_scalar(bn2[:, :, 1], bn2[:, :, 1], LN_EPS, None, ALU.add).then_inc(bn_done, 1)
            for n in range(2, 6):
                level(n)
            dve.wait_ge(ln_sd, 1)
            link(dve.reciprocal(ln_r[:, :], ln_r[:, :]))
            for t in range(NT):
                for g in range(G):
                    n = t * G + g
                    last = dve.tensor_scalar(v_tok[:, t, g * C:(g + 1) * C], v_tok[:, t, g * C:(g + 1) * C],
                                             bn2[:, n, 0:1], ln_r[:, n:n + 1], ALU.subtract, ALU.mult)
                last.then_inc(ln_norm, 1)
            level(6)
            level(7)
            for g in range(G):
                dve.wait_ge(mixed_done, g + 1)
                dve.wait_ge(z_out, NZ)
                dve.wait_ge(wsT_ready, 1)
                u = y_sb[:, :, HALF + g * C:HALF + (g + 1) * C]
                dve.scalar_tensor_tensor(out=u, in0=bank[:, 3 + g % 2, :].rearrange("p (n c) -> p n c", n=NT),
                                         scalar=bsT[:, g:g + 1], in1=u, op0=ALU.add, op1=ALU.mult)\
                   .then_inc(u_ready, 1)
            dve.wait_ge(f_merged, LEVELS * G)
            for h in range(G):
                dve.wait_ge(upd_done, h + 1)
                ub = bank[:, h % 2, :].rearrange("p (c v) -> p c v", c=NT)
                link(dve.tensor_copy(states[:, h, 0, :], ub[:, 0, :]))
                for c in range(1, NT - 1):
                    ins = dve.scalar_tensor_tensor(out=states[:, h, c, :], in0=states[:, h, c - 1, :],
                                                   scalar=fT[:, h, (c + 1) * C - 1:(c + 1) * C],
                                                   in1=ub[:, c, :], op0=ALU.mult, op1=ALU.add)
                    if c < NT - 2:
                        link(ins)
                    else:
                        ins.then_inc(state_ready, 1)
            for h in range(G):
                dve.wait_ge(o_sq, h + 1)
                dve.reduce_sum(o_ss[:, h, :], squares[:, h % 2, :].rearrange("p (c v) -> p c v", c=NT), axis=AX)\
                   .then_inc(o_ms, 1)
            dve.wait_ge(o_ms, G)
            dve.tensor_scalar(o_ss[:, :, :], o_ss[:, :, :], 1.0 / C, RMS_EPS, ALU.mult, ALU.add).then_inc(o_ms, 1)
            dve.wait_ge(o_sd, 1)
            link(dve.reciprocal(o_r[:, :, :], o_r[:, :, :]))
            dve.wait_ge(gg_ready, NT)
            for c in range(NT):
                for h in range(G):
                    gt = y_sb[:, c, h * C:(h + 1) * C]
                    last = dve.scalar_tensor_tensor(out=gt, in0=bank[:, [2, 7, 3, 4][h], c * C:(c + 1) * C],
                                                    scalar=o_r[:, h, c:c + 1], in1=gt, op0=ALU.mult, op1=ALU.mult)
                last.then_inc(y_ready, 1)

            def h2T_out(t):
                dve.wait_ge(h2T_done, t + 1)
                dve.tensor_copy(hT[:, 4:8, t * P:(t + 1) * P], bank[:, 7, :].rearrange("p (k t) -> p k t", k=4))\
                   .then_inc(h2T_d, 1)

            for t in range(NT):
                dve.wait_ge(yT_done, t + 1)
                dve.tensor_copy(hT[:, 4:8, t * P:(t + 1) * P], bank[:, 1, :].rearrange("p (k t) -> p k t", k=4))\
                   .then_inc(yT_d, 1)
                if t >= 1:
                    h2T_out(t - 1)
                for hf in range(2):
                    dve.wait_ge(wo_done, 2 * t + hf + 1)
                    last = dve.tensor_tensor(x_sb[:, t, hf * HALF:(hf + 1) * HALF],
                                             x_sb[:, t, hf * HALF:(hf + 1) * HALF], bank[:, 5 + hf, :], ALU.add)
                last.then_inc(x2_ready, 1)
                dve.wait_ge(x2_ss, t + 1)
                dve.tensor_scalar(stat_2[:, t, 1:2], stat_2[:, t, 0:1], 1.0 / D, RMS_EPS, ALU.mult, ALU.add)\
                   .then_inc(x2_ms, 1)
                dve.wait_ge(x2_sd, t + 1)
                link(dve.reciprocal(stat_2[:, t, 3:4], stat_2[:, t, 2:3]))
                dve.scalar_tensor_tensor(out=h2[:, t, :], in0=x_sb[:, t, :], scalar=stat_2[:, t, 3:4],
                                         in1=gain_ffn[:, :], op0=ALU.mult, op1=ALU.mult).then_inc(h2_ready, 1)
            h2T_out(NT - 1)

            dve.wait_ge(logit_done, NT)
            link(dve.tensor_copy(logits, bank[:, 4, 0:NT * NL].rearrange("p (t e) -> p t e", t=NT)))
            lg, le = logits[:, :, 0:NG], logits[:, :, NG:NL]
            link(dve.reduce_max(g_max[:, :, 0], lg, axis=AX))
            dve.tensor_tensor(g_exp, lg, g_max.to_broadcast([P, NT, NG]), ALU.subtract).then_inc(r_dve, 1)
            link(dve.tensor_tensor(g_hot, lg, g_max.to_broadcast([P, NT, NG]), ALU.is_equal))
            link(dve.tensor_tensor(g_pick, g_hot, first_w[:, :].unsqueeze(1).to_broadcast([P, NT, NG]), ALU.mult))
            link(dve.reduce_max(g_max[:, :, 0], g_pick, axis=AX))
            link(dve.tensor_tensor(g_hot, g_pick, g_max.to_broadcast([P, NT, NG]), ALU.is_equal))
            link(dve.memset(e_log, LOWEST))
            for t in range(NT):
                last = dve.copy_predicated(
                    e_log[:, t].rearrange("p (g e) -> p g e", g=NG),
                    g_hot[:, t].unsqueeze(2).to_broadcast([P, NG, EPG]).bitcast(I32),
                    le[:, t].rearrange("p (g e) -> p g e", g=NG))
            link(last)
            for t in range(NT):
                last = dve.max(top8[:, t], e_log[:, t])
            link(last)
            for t in range(NT):
                last = dve.max_index(idx8[:, t].bitcast(U32), top8[:, t], e_log[:, t])
            link(last)
            dve.tensor_tensor(gap, top8[:, :, 1], top8[:, :, 0], ALU.subtract).then_inc(r_dve, 1)
            link(dve.tensor_copy(top_i, idx8[:, :, 0:2].bitcast(U32)))
            hot_v = hot.rearrange("p t j e -> p (t j) e")
            link(dve.tensor_tensor(hot_v, iota_e[:, :].unsqueeze(1).to_broadcast([P, NT * 2, NE]),
                                   top_i.rearrange("p t j -> p (t j)").unsqueeze(2)
                                   .to_broadcast([P, NT * 2, NE]), ALU.is_equal))
            dve.tensor_tensor(hot_b[:, :, :], hot[:, :, 0, :], hot[:, :, 1, :], ALU.add).then_inc(rank_ops, 1)
            for kind in range(2):
                for parity in range(2):
                    last = dve.tensor_tensor(
                        deal[:, :, parity, kind, :], hot_v.rearrange("p n (q r) -> p n q r", r=2)[:, :, :, parity],
                        row_f[:, kind].rearrange("p t j -> p (t j)").unsqueeze(2)
                        .to_broadcast([P, NT * 2, PAIRS]), ALU.mult)
            last.then_inc(deal_ready, 1)
            dve.wait_ge(r_act, 1)
            link(dve.reduce_sum(g_sum, g_exp, axis=AX))
            dve.wait_ge(r_act, 2)
            link(dve.tensor_scalar(den, egap, 1.0, None, ALU.add))
            link(dve.tensor_tensor(den, den, g_sum, ALU.mult))
            link(dve.reciprocal(w_top[:, 0, :], den))
            dve.tensor_tensor(w_top[:, 1, :], w_top[:, 0, :], egap, ALU.mult)
            dve.wait_ge(rank_done, 1)
            rk = bank[:, 5, 0:NT * NE].rearrange("p (t e) -> p t e", t=NT)
            for j in range(2):
                last = dve.tensor_tensor(rank_all[:, :, j, :], hot[:, :, j, :], rk, ALU.mult)
            link(last)
            link(dve.reduce_sum(rank, rank_all.rearrange("p t j e -> p (t j) e"), axis=AX))

            def slots_of(c):
                dve.tensor_scalar(round_rank, rank, float(-c * RANKS), None, ALU.add).then_inc(s_dve, 1)
                n_link[0] += 1
                dve.wait_ge(s_dve, n_link[0])
                dve.tensor_tensor(in_round[:, c % 2, :, 0:RANKS],
                                  iota_s[:, 0:RANKS].unsqueeze(1).to_broadcast([P, NT * 2, RANKS]),
                                  round_rank.unsqueeze(2).to_broadcast([P, NT * 2, RANKS]), ALU.is_equal)\
                   .then_inc(round_ready, 1)

            def table_of(c):
                dve.wait_ge(slots_done, c + 1)
                dve.tensor_scalar(tab[:, :, c * PAIRS:(c + 1) * PAIRS],
                                  bank[:, 6 + c % 2, 0:2 * PAIRS].rearrange("p (k q) -> p k q", k=2),
                                  float(EMPTY), None, ALU.add).then_inc(tab_ready, 1)

            if RANKS < SLOTS:
                link(dve.memset(in_round, 0.0))
            slots_of(0)
            link(dve.reduce_max(most, bank[:, 5, NT * NE:(NT + 1) * NE], axis=AX))
            link(dve.tensor_scalar(over, limits[:, :], most, None, ALU.is_lt))
            link(dve.reduce_sum(most, over, axis=AX))
            dve.tensor_scalar(steps[:, :], most, float(PAIRS // 2), float(PAIRS // 2), ALU.mult,
                              ALU.subtract).then_inc(steps_ready, 1)
            table_of(0)
            for c in range(1, ROUNDS):
                slots_of(c)
                table_of(c)

            dve.wait_ge(steps_ready, 1)
            n_double = double_steps(dve)

            def gathered_T(n):
                dve.wait_ge(hgT_done, n)
                dve.tensor_copy(hgT[:, 4:8, :], bank[:, 4, :].rearrange("p (k s) -> p k s", k=4)).then_inc(hgT_d, 1)

            def hidden(n):
                dve.wait_ge(silu_done, n)
                dve.tensor_tensor(hid, silu_g, bank[:, 0, F:2 * F], ALU.mult).then_inc(hid_ready, 1)

            def rows_out(b, n, uses):
                dve.wait_ge(down_done, n)
                if uses is not None:
                    dve.wait_ge(scattered[b], uses)
                dve.tensor_copy(yo[b][:, HALF:D], bank[:, 2, :]).then_inc(yo_d, 1)

            gathered_T(1)
            hidden(1)
            gathered_T(2)
            hidden(2)
            rows_out(0, 1, None)
            gathered_T(3)
            hidden(3)
            rows_out(1, 2, None)
            gathered_T(4)
            with dve.Fori(1, n_double - 1) as i:
                for b in (1, 0):
                    o = 1 if b else 2
                    hidden(i * 2 + (o + 1))
                    rows_out(1 - b, i * 2 + o, i * 16)
                    gathered_T(i * 2 + (o + 2))
            hidden(n_double * 2)
            rows_out(0, n_double * 2 - 1, n_double * 16 - 16)
            rows_out(1, n_double * 2, n_double * 16 - 16)

            for t in range(NT):
                dve.wait_ge(er_loaded[t % 2], 16 * (t // 2 + 1))
                link(dve.scalar_tensor_tensor(out=x_sb[:, t, :], in0=er[t % 2][:, 0, :], scalar=w_top[:, 0, t:t + 1],
                                              in1=x_sb[:, t, :], op0=ALU.mult, op1=ALU.add))
                dve.scalar_tensor_tensor(out=x_sb[:, t, :], in0=er[t % 2][:, 1, :], scalar=w_top[:, 1, t:t + 1],
                                         in1=x_sb[:, t, :], op0=ALU.mult, op1=ALU.add).then_inc(f_y, 1)
                dve.wait_ge(f_ss, t + 1)
                dve.tensor_scalar(stat_f[:, t, 1:2], stat_f[:, t, 0:1], 1.0 / D, RMS_EPS, ALU.mult, ALU.add)\
                   .then_inc(f_ms, 1)
                dve.wait_ge(f_sd, t + 1)
                link(dve.reciprocal(stat_f[:, t, 3:4], stat_f[:, t, 2:3]))
                dve.wait_ge(fin_loaded, 16)
                dve.scalar_tensor_tensor(out=y_sb[:, t, :], in0=x_sb[:, t, :], scalar=stat_f[:, t, 3:4],
                                         in1=gain_fin, op0=ALU.mult, op1=ALU.mult).then_inc(f_out, 1)

        @block.tensor
        def _(pe):
            def transposes(dst, src_of, n, done):
                for a in range(n):
                    last = pe.transpose(dst(a), src_of(a), ident[:, :])
                last.then_inc(done, 1)

            pe.wait_ge(s_const, 1)
            pe.wait_ge(xn_ready, NT)
            for k in range(KD):
                if k >= 2:
                    pe.wait_ge(hT_even if k % 2 == 0 else hT_odd, k // 2)
                transposes(lambda t: bank[:, 3 + k % 2, t * P:(t + 1) * P], lambda t: y_sb[:, t, k:D:KD], NT, xT_done)
            pe.wait_ge(s_const, 2)
            for g in range(G):
                pe.transpose(bank[:, 5, g * C:(g + 1) * C], ws_raw[:, g, :], ident[:, :])
            pe.transpose(bank[:, 6, 0:G], bs_raw[:, :], ident[0:G, 0:G]).then_inc(wsT_done, 1)

            def scores(n):
                for h in range(G):
                    u = n * G + h
                    if u < 2:
                        pe.wait_ge(wsT_ready, 1)
                    else:
                        pe.wait_ge(attn_kept, u - 1)
                    if n == 0:
                        pe.wait_ge(z_out, G + h + 1)
                        pe.wait_ge(fk_ready, h + 1)
                    else:
                        pe.wait_ge(decayed, u - G + 1)
                    for c in range(NT):
                        last = pe.matmul(bank[:, 5 + h % 2, c * C:(c + 1) * C], kT[:, h, c * C:(c + 1) * C],
                                         qT[:, h, c * C:(c + 1) * C], start=True, stop=True)
                    last.then_inc(attn_done, 1)

            pe.wait_ge(hT_even, KD // 2)
            pe.wait_ge(hT_odd, KD // 2)
            for j in range(NZ):
                blk, t = divmod(j, NT)
                wb = a_ring[:, blk % 2, :].rearrange("p (k n) -> p k n", k=KD)
                if t == 0:
                    pe.wait_ge(s_ring[blk % 2], 16 * (blk // 2 + 1))
                if j >= Z_BANKS:
                    pe.wait_ge(z_out, j - Z_BANKS + 1)
                for k in range(KD):
                    if blk < 2:
                        lhsT, rhs = wb[:, k, t * P:(t + 1) * P], hT[:, k, :]
                    else:
                        lhsT, rhs = hT[:, k, t * P:(t + 1) * P], wb[:, k, :]
                    last = pe.matmul(bank[:, j % Z_BANKS, :], lhsT, rhs, start=(k == 0), stop=(k == KD - 1))
                last.then_inc(z_done, 1)
                if j in LEVEL_AT:
                    scores(LEVEL_AT.index(j))
            pe.wait_ge(vn_ready, NT)
            for g in range(G):
                if g >= 2:
                    pe.wait_ge(u_ready, g - 1)
                pe.matmul(bank[:, 3 + g % 2, :].rearrange("p (n c) -> p n c", n=NT), wsT[:, g, :],
                          v_tok[:, :, g * C:(g + 1) * C], start=True, stop=True).then_inc(mixed_done, 1)
            for h in range(G):
                pe.wait_ge(decayed, LEVELS * G + h + 1)
                if h < 2:
                    pe.wait_ge(attn_kept, (LEVELS + 1) * G)
                else:
                    pe.wait_ge(kt_ready, h - 1)
                transposes(lambda c: bank[:, 5 + h % 2, c * C:(c + 1) * C], lambda c: kT[:, h, c * C:(c + 1) * C],
                           NT, kt_done)
            for h in range(G):
                pe.wait_ge(kt_ready, h + 1)
                pe.wait_ge(z_out, NZ)
                if h >= 2:
                    pe.wait_ge(state_ready, h - 1)
                for c in range(NT - 1):
                    last = pe.matmul(bank[:, h % 2, c * C:(c + 1) * C], k_tok[:, h, c, :],
                                     i_tok[:, c, h * C:(h + 1) * C], start=True, stop=True)
                last.then_inc(upd_done, 1)
            for h in range(G):
                ob = [2, 7, 3, 4][h]
                pe.wait_ge(u_ready, G)
                pe.wait_ge(state_ready, h + 1)
                for c in range(NT):
                    last = pe.matmul(bank[:, ob, c * C:(c + 1) * C], attn[:, h, c, :],
                                     i_tok[:, c, h * C:(h + 1) * C], start=True, stop=(c == 0))
                    if c:
                        last = pe.matmul(bank[:, ob, c * C:(c + 1) * C], qT[:, h, c * C:(c + 1) * C],
                                         states[:, h, c - 1, :], start=False, stop=True)
                last.then_inc(o_done, 1)

            def h2_T(t):
                pe.wait_ge(h2_ready, t + 1)
                if t >= 1:
                    pe.wait_ge(h2T_a, t)
                    pe.wait_ge(h2T_d, t)
                transposes(lambda k: bank[:, 2 if k < 4 else 7, (k % 4) * P:(k % 4 + 1) * P],
                           lambda k: h2[:, t, k:D:KD], KD, h2T_done)

            def route(t):
                pe.wait_ge(h2T_a, t + 1)
                pe.wait_ge(h2T_d, t + 1)
                for k in range(KD):
                    last = pe.matmul(bank[:, 4, t * NL:(t + 1) * NL], hT[:, k, t * P:(t + 1) * P], wr[:, k, :],
                                     start=(k == 0), stop=(k == KD - 1))
                last.then_inc(logit_done, 1)

            pe.wait_ge(s_ring[0], 16 * 4)
            pe.wait_ge(s_ring[1], 16 * 4)
            pe.wait_ge(y_ready, NT)
            for t in range(NT):
                if t >= 1:
                    pe.wait_ge(yT_a, t)
                    pe.wait_ge(yT_d, t)
                transposes(lambda k: bank[:, k // 4, (k % 4) * P:(k % 4 + 1) * P],
                           lambda k: y_sb[:, t, k:D:KD], KD, yT_done)
                if t >= 1:
                    pe.wait_ge(x2_ready, t)
                pe.wait_ge(yT_a, t + 1)
                pe.wait_ge(yT_d, t + 1)
                for hf in range(2):
                    wb = a_ring[:, hf, :].rearrange("p (k n) -> p k n", k=KD)
                    for k in range(KD):
                        last = pe.matmul(bank[:, 5 + hf, :], hT[:, k, t * P:(t + 1) * P], wb[:, k, :],
                                         start=(k == 0), stop=(k == KD - 1))
                    last.then_inc(wo_done, 1)
                if t >= 1:
                    h2_T(t - 1)
                    route(t - 1)
            h2_T(NT - 1)
            route(NT - 1)

            pe.wait_ge(rank_ops, 1)
            for t in range(NT + 1):
                cols = bank[:, 5, t * NE:(t + 1) * NE]
                for s in range(min(t + 1, NT)):
                    last = pe.matmul(cols, before_b[:, :] if s == t else ones_b[:, :], hot_b[:, s, :],
                                     start=(s == 0), stop=(s == min(t, NT - 1)))
            last.then_inc(rank_done, 1)
            pe.wait_ge(deal_ready, 1)
            for c in range(ROUNDS):
                pe.wait_ge(round_ready, c + 1)
                if c >= 2:
                    pe.wait_ge(tab_ready, c - 1)
                for n in range(2 * NT):
                    for parity in range(2):
                        last = pe.matmul(bank[parity * SLOTS:(parity + 1) * SLOTS, 6 + c % 2, 0:2 * PAIRS],
                                         in_round[:, c % 2, n, :],
                                         deal[:, n, parity].rearrange("p k q -> p (k q)"),
                                         start=(n == 0), stop=(n == 2 * NT - 1))
                last.then_inc(slots_done, 1)

            pe.wait_ge(steps_ready, 1)
            n_double = double_steps(pe)

            def gathered_T(b, uses):
                pe.wait_ge(gathered[b], uses)
                transposes(lambda k: bank[:, 3 + k // 4, (k % 4) * P:(k % 4 + 1) * P],
                           lambda k: hg[b][:, k:D:KD], KD, hgT_done)

            def gate_up(b, n, uses):
                pe.wait_ge(hgT_a, n)
                pe.wait_ge(hgT_d, n)
                pe.wait_ge(wgu_loaded[b], uses * 2)
                for k in range(KD):
                    for e in range(2):
                        w = wgu[b][:, e].rearrange("p g (k f) -> p g k f", k=KD)
                        last = pe.matmul(
                            bank[e * SLOTS:(e + 1) * SLOTS, 0, :].rearrange("p (g f) -> p g f", g=2),
                            hgT[:, k, e * SLOTS:(e + 1) * SLOTS], w[:, :, k, :],
                            start=(k == 0), stop=(k == KD - 1))
                last.then_inc(gu_done, 1)

            def hidden_T(n):
                pe.wait_ge(hid_ready, n)
                transposes(lambda k: bank[:, 5, k * P:(k + 1) * P], lambda k: hid[:, k:F:KF], KF, hidT_done)

            def down(b, n, uses, prev):
                pe.wait_ge(hidT_ready, n)
                if prev is not None:
                    pe.wait_ge(yo_a, prev)
                    pe.wait_ge(yo_d, prev)
                pe.wait_ge(wd_loaded[b], uses)
                for hf in range(2):
                    for k in range(KF):
                        for e in range(2):
                            w = wd[b][:, e].rearrange("p (k d) -> p k d", k=KF)
                            last = pe.matmul(bank[e * SLOTS:(e + 1) * SLOTS, 1 + hf, :],
                                             hidT[:, k, e * SLOTS:(e + 1) * SLOTS],
                                             w[:, k, hf * HALF:(hf + 1) * HALF],
                                             start=(k == 0), stop=(k == KF - 1))
                last.then_inc(down_done, 1)

            gathered_T(0, 16)
            gate_up(0, 1, 16)
            gathered_T(1, 16)
            hidden_T(1)
            gate_up(1, 2, 16)
            down(0, 1, 16, None)
            gathered_T(0, 32)
            hidden_T(2)
            gate_up(0, 3, 32)
            down(1, 2, 16, 1)
            gathered_T(1, 32)
            hidden_T(3)
            with pe.Fori(1, n_double - 1) as i:
                gate_up(1, i * 2 + 2, i * 16 + 16)
                down(0, i * 2 + 1, i * 16 + 16, i * 2)
                gathered_T(0, i * 16 + 32)
                hidden_T(i * 2 + 2)
                gate_up(0, i * 2 + 3, i * 16 + 32)
                down(1, i * 2 + 2, i * 16 + 16, i * 2 + 1)
                gathered_T(1, i * 16 + 32)
                hidden_T(i * 2 + 3)
            gate_up(1, n_double * 2, n_double * 16)
            down(0, n_double * 2 - 1, n_double * 16, n_double * 2 - 2)
            hidden_T(n_double * 2)
            down(1, n_double * 2, n_double * 16, n_double * 2 - 1)


_INS = ["x", "norm_mix", "w_in", "hgrn_norm", "tmlp_ln_g", "tmlp_ln_b", "w_spatial", "b_spatial", "w_out",
        "norm_ffn", "w_router_group", "w_router_expert", "w_gate", "w_up", "w_down", "norm_final"]


def kernel(**inputs):
    import numpy as np
    import concourse.bacc as bacc
    from concourse.bass_utils import run_bass_kernel_spmd

    nc = bacc.Bacc("TRN2", target_bir_lowering=False, num_devices=1)
    arrays, args = {}, []
    for name in _INS:
        a = np.ascontiguousarray(inputs[name])
        if name != "norm_final":
            a = a.reshape(a.shape[1:])
        arrays[name + "_in"] = a
        args.append(nc.dram_tensor(name + "_in", a.shape, F32, kind="ExternalInput").ap())
    out = nc.dram_tensor("out", arrays["x_in"].shape, F32, kind="ExternalOutput").ap()
    hybrid_trunk(nc, *args, out)
    r = run_bass_kernel_spmd(nc, [arrays], core_ids=[0])
    return r.results[0]["out"].reshape(np.shape(inputs["x"]))
```

```python
from contextlib import ExitStack

import concourse.bass as bass
from concourse import mybir

ALU = mybir.AluOpType
ACT = mybir.ActivationFunctionType
AX = mybir.AxisListType.X
F32 = mybir.dt.float32
BF16 = mybir.dt.bfloat16
I32 = mybir.dt.int32
U32 = mybir.dt.uint32

P = 128
RMS_EPS = 1e-6
LN_EPS = 1e-5
F_FLOOR = 1e-30
SLOTS = 64
EMPTY = 4096
LOWEST = -3.0e38


def hybrid_trunk(nc, x, norm_mix, w_in, hgrn_norm, ln_g, ln_b, w_spatial, b_spatial, w_out,
                 norm_ffn, w_rg, w_re, w_gate, w_up, w_down, norm_final, out):
    T, D = x.shape
    NT, KD = T // P, D // P
    G = w_spatial.shape[0]
    C = w_spatial.shape[1]
    NG = w_rg.shape[1]
    NE = w_re.shape[1]
    EPG = NE // NG
    F = w_gate.shape[2]
    KF = F // P
    NL = NG + NE
    HALF = D // 2
    PAIRS = NE // 2
    ROUNDS = T // SLOTS
    LEVELS = C.bit_length() - 1
    assert G * C == HALF and C == P and F == 2 * P and NT == 4 and SLOTS * 2 == P
    assert w_in.shape[1] == 6 * HALF and PAIRS % 2 == 0

    h2_rows = nc.dram_tensor("h2_rows", (T, D), F32, kind="Internal").ap()
    expert_rows = nc.dram_tensor("expert_rows", (2 * T, D), F32, kind="Internal").ap()

    w_in_v = w_in.rearrange("(p k) e -> p k e", k=KD)
    w_out_v = w_out.rearrange("(p k) e -> p k e", k=KD)

    with ExitStack() as ctx:
        def sb(name, shape, dt=F32):
            return ctx.enter_context(nc.sbuf_tensor(name, shape, dt))

        def sem(name):
            return ctx.enter_context(nc.semaphore(name))

        x_sb = sb("x_sb", [P, NT, D])
        a_hT = sb("a_hT", [P, KD * T])
        a_ring = sb("a_ring", [P, 2, KD * HALF])
        qT = sb("qT", [P, G, T])
        fT = sb("fT", [P, G, T])
        kT = sb("kT", [P, G, T])
        a_iv = sb("a_iv", [P, 2, NT, HALF])
        y_sb = sb("y_sb", [P, NT, D])
        a_ak = sb("a_ak", [P, 2, G, NT, C])
        wgu0 = sb("wgu0", [P, 2, 2, KD * F])
        wd0 = sb("wd0", [P, 2, KF * D])

        hT = a_hT[:, :].rearrange("p (k t) -> p k t", k=KD)
        states = a_hT[:, 0:G * (NT - 1) * C].rearrange("p (h c v) -> p h c v", h=G, c=NT - 1)
        squares = a_hT[:, 2048:2048 + 2 * HALF].rearrange("p (b n) -> p b n", b=2)
        junk = a_ak[:, :, :, :, :].rearrange("p a h c v -> p (a h c v)").rearrange("p (t d) -> p t d", t=NT)
        junk_last = a_ring[:, 0, :].rearrange("p (t d) -> p t d", t=NT)
        i_tok, v_tok = a_iv[:, 0], a_iv[:, 1]
        h2 = a_iv[:, :, :, :].rearrange("p a t n -> p (a t n)").rearrange("p (t d) -> p t d", t=NT)
        attn, k_tok = a_ak[:, 0], a_ak[:, 1]
        wgu = [wgu0[:, :, :, :], a_ring[:, :, :].rearrange("p e (g n) -> p e g n", g=2)]
        wd = [wd0[:, :, :], a_hT[:, :].rearrange("p (e n) -> p e n", e=2)]
        hg = [qT[:, :, :].rearrange("p h t -> p (h t)")[:, b * D:(b + 1) * D] for b in range(2)]
        fT_flat = fT[:, :, :].rearrange("p h t -> p (h t)")
        hgT = fT_flat[:, 0:KD * P].rearrange("p (k s) -> p k s", k=KD)
        silu_g = fT_flat[:, KD * P:KD * P + F]
        hid = fT_flat[:, KD * P + F:KD * P + 2 * F]
        hidT = fT_flat[:, KD * P + 2 * F:KD * P + 3 * F].rearrange("p (k s) -> p k s", k=KF)
        yo = [kT[:, :, :].rearrange("p h t -> p (h t)")[:, b * D:(b + 1) * D] for b in range(2)]
        er = [wgu0[:, t // 2, t % 2, :].rearrange("p (j d) -> p j d", j=2) for t in range(NT)]

        ident = sb("ident", [P, P])
        ones_b = sb("ones_b", [P, P], BF16)
        before_b = sb("before_b", [P, P], BF16)
        level_mask = sb("level_mask", [P, LEVELS, C])
        gain_mix = sb("gain_mix", [P, KD])
        gnorm = sb("gnorm", [P, C])
        lng = sb("lng", [P, HALF])
        lnb = sb("lnb", [P, HALF])
        ws_raw = sb("ws_raw", [P, G, C])
        wsT = sb("wsT", [P, G, C])
        bs_raw = sb("bs_raw", [G, C])
        bsT = sb("bsT", [P, G])
        gain_ffn = sb("gain_ffn", [P, D])
        wr_g = sb("wr_g", [P, KD, NG])
        wr_e = sb("wr_e", [P, KD, NE])
        wr = sb("wr", [P, KD, NL])
        stat_x, stat_2, stat_f = (sb(n, [P, NT, 4]) for n in ("stat_x", "stat_2", "stat_f"))
        bn6 = sb("bn6", [P, NT, G, 6])
        bn2 = sb("bn2", [P, NT * G, 2])
        ln_r = sb("ln_r", [P, NT * G])
        o_ss = sb("o_ss", [P, G, NT])
        o_r = sb("o_r", [P, G, NT])
        tab = sb("tab", [P, 2, ROUNDS * PAIRS], I32)
        cur = sb("cur", [P, 4], I32)
        steps = sb("steps", [P, 1], I32)
        w_top = sb("w_top", [P, 2, NT])

        rt_flat = a_ak[:, :, :, :, :].rearrange("p a h c v -> p (a h c v)")
        rt_used = [0]

        def rt(*shape):
            n = 1
            for s in shape:
                n *= s
            v = rt_flat[:, rt_used[0]:rt_used[0] + n]
            rt_used[0] += n
            assert rt_used[0] <= 2 * G * NT * C
            if len(shape) == 2:
                return v.rearrange("p (a b) -> p a b", a=shape[0])
            if len(shape) == 3:
                return v.rearrange("p (a b c) -> p a b c", a=shape[0], b=shape[1])
            if len(shape) == 4:
                return v.rearrange("p (a b c d) -> p a b c d", a=shape[0], b=shape[1], c=shape[2])
            return v

        logits = rt(NT, NL)
        g_max = rt(NT, 1)
        g_exp = rt(NT, NG)
        g_sum = rt(NT)
        p_sel = rt(NT)
        g_pick = rt(NT, NG)
        g_hot = rt(NT, NG)
        e_log = rt(NT, NE)
        top8 = rt(NT, 8)
        idx8 = rt(NT, 8)
        top_i = rt(NT, 2)
        gap = rt(NT)
        egap = rt(NT)
        den = rt(NT)
        hot = rt(NT, 2, NE)
        rank_all = rt(NT, 2, NE)
        rank = rt(NT * 2)
        round_rank = rt(NT * 2)
        deal = rt(NT * 2, 2, 2, PAIRS)
        in_round = rt(2, NT * 2, SLOTS)
        most = rt(1)
        over = rt(ROUNDS)
        gain_fin = rt(D)
        hot_b = sb("hot_b", [P, NT, NE], BF16)
        iota_e = sb("iota_e", [P, NE])
        iota_s = sb("iota_s", [P, SLOTS])
        iota_i = sb("iota_i", [P, SLOTS], I32)
        row_i = sb("row_i", [P, 2, NT, 2], I32)
        row_f = sb("row_f", [P, 2, NT, 2])
        first_w = sb("first_w", [P, NG])
        limits = sb("limits", [P, ROUNDS])

        bank = ctx.enter_context(nc.psum_tensor("bank", [P, 8, HALF], F32))

        s_x = [sem(f"x_loaded{t}") for t in range(NT)]
        s_gain = sem("gain_mix_loaded")
        s_small = sem("small_loaded")
        s_ring = [sem(f"ring_loaded{b}") for b in range(2)]
        s_const = sem("const_made")
        s_cstep = sem("const_step")
        x_ss = sem("x_ss")
        x_ms = sem("x_ms")
        x_sd = sem("x_sd")
        xn_ready = sem("xn_ready")
        xT_done = sem("xT_done")
        hT_even = sem("hT_even")
        hT_odd = sem("hT_odd")
        wsT_done = sem("wsT_done")
        wsT_ready = sem("wsT_ready")
        z_done = sem("z_done")
        z_out = sem("z_out")
        fk_ready = sem("fk_ready")
        attn_done = sem("attn_done")
        attn_kept = sem("attn_kept")
        decayed = sem("decayed")
        f_merged = sem("f_merged")
        bn_done = sem("bn_done")
        ln_sd = sem("ln_sd")
        ln_norm = sem("ln_norm")
        vn_ready = sem("vn_ready")
        gg_ready = sem("gg_ready")
        mixed_done = sem("mixed_done")
        u_ready = sem("u_ready")
        kt_done = sem("ktok_done")
        kt_ready = sem("ktok_ready")
        upd_done = sem("update_done")
        state_ready = sem("state_ready")
        o_done = sem("o_done")
        o_sq = sem("o_sq")
        o_ms = sem("o_ms")
        o_sd = sem("o_sd")
        y_ready = sem("y_ready")
        T_done = sem("transposed_done")
        T_a = sem("transposed_act")
        T_d = sem("transposed_dve")
        wo_done = sem("w_out_done")
        x2_ready = sem("x2_ready")
        x2_ss = sem("x2_ss")
        x2_ms = sem("x2_ms")
        x2_sd = sem("x2_sd")
        h2_ready = sem("h2_ready")
        h2_stored = sem("h2_stored")
        logit_done = sem("logits_done")
        r_dve = sem("router_dve")
        r_act = sem("router_act")
        rank_ops = sem("rank_ops")
        rank_done = sem("rank_done")
        steps_ready = sem("steps_ready")
        deal_ready = sem("deal_ready")
        round_ready = sem("round_ready")
        slots_done = sem("slots_done")
        tab_ready = sem("tab_ready")
        later_step = sem("later_step")
        hg_clear = sem("hg_clear")
        wgu_loaded = [sem(f"wgu_loaded{b}") for b in range(2)]
        wd_loaded = [sem(f"wd_loaded{b}") for b in range(2)]
        cur_ready = sem("cur_ready")
        gathered = [sem(f"gathered{b}") for b in range(2)]
        scattered = [sem(f"scattered{b}") for b in range(2)]
        hgT_done = sem("hgT_done")
        hgT_a = sem("hgT_act")
        hgT_d = sem("hgT_dve")
        gu_done = sem("gate_up_done")
        silu_done = sem("silu_done")
        hid_ready = sem("hid_ready")
        hidT_done = sem("hidT_done")
        hidT_ready = sem("hidT_ready")
        down_done = sem("down_done")
        yo_a = sem("yo_act")
        yo_d = sem("yo_dve")
        er_loaded = [sem(f"er_loaded{t}") for t in range(NT)]
        fin_loaded = sem("gain_fin_loaded")
        f_dve = sem("final_dve")
        f_y = sem("final_y")
        f_ss = sem("final_ss")
        f_ms = sem("final_ms")
        f_sd = sem("final_sd")
        f_out = sem("final_out")
        out_stored = sem("out_stored")
        s_dve = sem("dve_step")

        block = ctx.enter_context(nc.Block())

        SMALL = 8
        BLOCKS = 8
        NZ = 6 * NT
        COL = [1, 0, 5, 2, 3, 4]
        LEVEL_AT = [2 * NT + 2 * n for n in range(LEVELS + 1)]
        Z_BANKS = 3
        Y_GROUP, H_GROUP = [0, 1, 2, 4], [3, 5, 6, 7]

        def more_steps(eng):
            return eng.value_load(steps[0:1, 0:1], min_val=0, max_val=(ROUNDS - 1) * PAIRS // 2)

        def double_steps(eng):
            return more_steps(eng) + PAIRS // 2

        def pair_w(w, q):
            return w[q * 2:q * 2 + 2] if isinstance(q, int) else w[bass.ds(q * 2, 2)]

        def load_gate_up(sp, b, q):
            for g, w in enumerate((w_gate, w_up)):
                sp.dma_start(wgu[b][:, :, g, :],
                             pair_w(w, q).rearrange("e (p k) f -> p e (k f)", k=KD)).then_inc(wgu_loaded[b], 16)

        def load_down(sp, b, q):
            sp.dma_start(wd[b], pair_w(w_down, q).rearrange("e (p k) d -> p e (k d)", k=KF))\
              .then_inc(wd_loaded[b], 16)

        @block.sync
        def _(sp):
            for t in range(NT):
                sp.dma_start(x_sb[:, t, :], x[t * P:(t + 1) * P, :]).then_inc(s_x[t], 16)
            for j in range(BLOCKS):
                src = w_in_v[:, :, COL[j] * HALF:(COL[j] + 1) * HALF] if j < 6 \
                    else w_out_v[:, :, (j - 6) * HALF:(j - 5) * HALF]
                if j >= 2:
                    sp.wait_ge(z_done, NT * (j - 1))
                sp.dma_start(a_ring[:, j % 2, :].rearrange("p (k n) -> p k n", k=KD), src)\
                  .then_inc(s_ring[j % 2], 16)
                if j == 2:
                    load_gate_up(sp, 0, 0)
                    load_down(sp, 0, 0)
            for t in range(NT):
                sp.wait_ge(h2_ready, t + 1)
                sp.dma_start(h2_rows[t * P:(t + 1) * P, :], h2[:, t, :]).then_inc(h2_stored, 16)
            sp.wait_ge(wo_done, 2 * NT)
            load_gate_up(sp, 1, 1)
            sp.wait_ge(logit_done, NT)
            load_down(sp, 1, 1)
            sp.wait_ge(steps_ready, 1)
            n_double = double_steps(sp)
            with sp.Fori(1, n_double) as m:
                for b in range(2):
                    q = (m % (PAIRS // 2)) * 2 + b
                    sp.wait_ge(gu_done, m * 2 + (b - 1))
                    load_gate_up(sp, b, q)
                    sp.wait_ge(down_done, m * 2 + (b - 1))
                    load_down(sp, b, q)
            for b in range(2):
                sp.wait_ge(scattered[b], n_double * 16)
            for t in range(NT):
                sp.dma_start(er[t], expert_rows[2 * t * P:2 * (t + 1) * P, :]
                             .rearrange("(p j) d -> p j d", j=2)).then_inc(er_loaded[t], 16)
            for t in range(NT):
                sp.wait_ge(f_out, t + 1)
                sp.dma_start(out[t * P:(t + 1) * P, :], y_sb[:, t, :]).then_inc(out_stored, 16)
            sp.wait_ge(out_stored, 16 * NT)

        @block.gpsimd
        def _(pool):
            made = [0]

            def step(ins):
                made[0] += 1
                ins.then_inc(s_cstep, 1)
                pool.wait_ge(s_cstep, made[0])

            step(pool.memset(ident[:, :], 0.0))
            pool.affine_select(out=ident[:, :], in_=ident[:, :], compare_op=ALU.not_equal, fill=1.0, base=0,
                               pattern=[[-1, P]], channel_multiplier=1).then_inc(s_const, 1)
            pool.wait_ge(s_small, 16 * SMALL)
            pool.affine_select(out=ws_raw[:, :, :], in_=ws_raw[:, :, :], compare_op=ALU.is_ge, fill=0.0, base=0,
                               pattern=[[0, G], [-1, C]], channel_multiplier=1).then_inc(s_const, 1)
            step(pool.memset(level_mask[:, :, :], 0.0))
            for n in range(LEVELS):
                h = 1 << n
                right = level_mask[:, n, :].rearrange("p (b two j) -> p b two j", two=2, j=h)[:, :, 1, :]
                nb = C // (2 * h)
                step(pool.memset(right, 1.0))
                step(pool.affine_select(out=right, in_=right, compare_op=ALU.is_ge, fill=0.0, base=0,
                                        pattern=[[-2 * h, nb], [0, h]], channel_multiplier=1))
                last = pool.affine_select(out=right, in_=right, compare_op=ALU.is_ge, fill=0.0, base=h - 1,
                                          pattern=[[2 * h, nb], [0, h]], channel_multiplier=-1)
            last.then_inc(s_const, 1)
            step(pool.memset(ones_b[:, :], 1.0))
            pool.affine_select(out=before_b[:, :], in_=ones_b[:, :], compare_op=ALU.is_gt, fill=0.0, base=0,
                               pattern=[[1, P]], channel_multiplier=-1).then_inc(s_const, 1)
            step(pool.iota(iota_i[:, :], pattern=[[1, SLOTS]], base=0, channel_multiplier=0))
            pool.tensor_copy(iota_e[:, :], iota_i[:, 0:NE])
            pool.tensor_copy(iota_s[:, :], iota_i[:, :])
            pool.iota(row_i[:, 0], pattern=[[P, NT], [0, 2]], base=-EMPTY, channel_multiplier=1)
            step(pool.iota(row_i[:, 1], pattern=[[2 * P, NT], [1, 2]], base=-EMPTY, channel_multiplier=2))
            pool.tensor_copy(row_f[:, :, :, :], row_i[:, :, :, :])
            pool.tensor_scalar(first_w[:, :], iota_i[:, 0:NG], -1.0, float(NG), ALU.mult, ALU.add)
            pool.tensor_scalar(limits[:, :], iota_i[:, 0:ROUNDS], float(SLOTS), 0.0, ALU.mult, ALU.add)
            pool.tensor_copy(wr[:, :, 0:NG], wr_g[:, :, :])
            pool.tensor_copy(wr[:, :, NG:NL], wr_e[:, :, :]).then_inc(s_const, 1)
            pool.wait_ge(ln_norm, NT)
            for t in range(NT):
                step(pool.tensor_tensor(v_tok[:, t, :], v_tok[:, t, :], lng[:, :], ALU.mult))
                pool.tensor_tensor(v_tok[:, t, :], v_tok[:, t, :], lnb[:, :], ALU.add).then_inc(vn_ready, 1)
            for t in range(NT):
                pool.wait_ge(z_out, 4 * NT + t + 1)
                gt = y_sb[:, t, 0:HALF].rearrange("p (h v) -> p h v", h=G)
                pool.tensor_tensor(gt, gt, gnorm[:, :].unsqueeze(1).to_broadcast([P, G, C]), ALU.mult)\
                    .then_inc(gg_ready, 1)
            pool.wait_ge(o_done, G)
            for b in range(2):
                pool.memset(hg[b], 0.0).then_inc(hg_clear, 1)

            pool.wait_ge(steps_ready, 1)
            extra = more_steps(pool)
            n_double = extra + PAIRS // 2
            pool.wait_ge(h2_stored, 16 * NT)
            pool.wait_ge(hg_clear, 2)

            def pick(kind, b, step_n, n):
                c = 2 * kind + b
                col = step_n if isinstance(step_n, int) else bass.ds(step_n, 1)
                src = tab[:, kind, col:col + 1] if isinstance(step_n, int) else tab[:, kind, col]
                pool.tensor_copy(cur[:, c:c + 1], src).then_inc(cur_ready, 1)
                pool.wait_ge(cur_ready, n)
                return cur[:, c:c + 1]

            def gather(b, step_n, n, limit):
                pool.indirect_dma_start(
                    hg[b], None, h2_rows, bass.IndirectOffsetOnAxis(ap=pick(0, b, step_n, n), axis=0),
                    bounds_check=limit(), oob_is_err=False).then_inc(gathered[b], 16)

            def scatter(b, step_n, n, limit):
                pool.indirect_dma_start(
                    expert_rows, bass.IndirectOffsetOnAxis(ap=pick(1, b, step_n, n), axis=0), yo[b], None,
                    bounds_check=limit(), oob_is_err=False).then_inc(scattered[b], 16)

            pool.wait_ge(tab_ready, 1)
            gather(0, 0, 1, lambda: T - 1)
            gather(1, 1, 2, lambda: T - 1)
            pool.wait_ge(hgT_done, 1)
            gather(0, 2, 3, lambda: T - 1)
            pool.wait_ge(yo_a, 1)
            pool.wait_ge(yo_d, 1)
            scatter(0, 0, 4, lambda: 2 * T - 1)
            pool.wait_ge(hgT_done, 2)
            gather(1, 3, 5, lambda: T - 1)
            with pool.If(extra > 0):
                pool.wait_ge(tab_ready, ROUNDS)
            with pool.Fori(2, n_double) as m:
                for b in range(2):
                    pool.wait_ge(yo_a, m * 2 + (b - 2))
                    pool.wait_ge(yo_d, m * 2 + (b - 2))
                    scatter(1 - b, m * 2 + (b - 3), m * 4 + (2 * b - 2),
                            lambda: pool.snap(m + (2 * T - 1 + b)))
                    pool.wait_ge(hgT_done, m * 2 + (b - 1))
                    gather(b, m * 2 + b, m * 4 + (2 * b - 1), lambda: pool.snap(m + (T - 1 + 4 * b)))
            for k in range(3):
                b = (k + 1) % 2
                pool.wait_ge(yo_a, n_double * 2 + (k - 2))
                pool.wait_ge(yo_d, n_double * 2 + (k - 2))
                scatter(b, n_double * 2 + (k - 3), n_double * 4 + (k - 2),
                        lambda: pool.snap(n_double + (2 * T - 1 + 8 * k)))

        @block.scalar
        def _(act):
            act.dma_start(gain_mix[:, :], norm_mix.rearrange("(p k) -> p k", k=KD)).then_inc(s_gain, 16)
            loads = [(ws_raw[:, :, :], w_spatial.rearrange("g t s -> t g s")),
                     (bs_raw[:, :], b_spatial),
                     (gnorm[:, :], hgrn_norm.unsqueeze(0).to_broadcast([P, C])),
                     (lng[:, :], ln_g.unsqueeze(0).to_broadcast([P, HALF])),
                     (lnb[:, :], ln_b.unsqueeze(0).to_broadcast([P, HALF])),
                     (gain_ffn[:, :], norm_ffn.unsqueeze(0).to_broadcast([P, D])),
                     (wr_g[:, :, :], w_rg.rearrange("(p k) e -> p k e", k=KD)),
                     (wr_e[:, :, :], w_re.rearrange("(p k) e -> p k e", k=KD))]
            assert len(loads) == SMALL
            for t in range(NT):
                act.wait_ge(s_x[t], 16)
                act.activation(junk[:, t, :], x_sb[:, t, :], ACT.Square, accum_out=stat_x[:, t, 0:1]).then_inc(x_ss, 1)
            act.wait_ge(x_ms, 1)
            act.activation(stat_x[:, :, 2], stat_x[:, :, 1], ACT.Sqrt).then_inc(x_sd, 1)
            for dst, src in loads:
                act.dma_start(dst, src).then_inc(s_small, 16)
            act.wait_ge(s_gain, 16)
            for k in range(0, KD, 2):
                act.wait_ge(xT_done, k + 1)
                act.activation(hT[:, k, :], bank[:, 3, :], ACT.Copy, scale=gain_mix[:, k:k + 1])\
                   .then_inc(hT_even, 1)
            act.wait_ge(wsT_done, 1)
            act.activation(wsT[:, :, :].rearrange("p g t -> p (g t)"), bank[:, 5, :], ACT.Copy)
            act.activation(bsT[:, :], bank[:, 6, 0:G], ACT.Copy).then_inc(wsT_ready, 1)
            for j in range(NZ):
                blk, t = divmod(j, NT)
                dst, fn = [(fT[:, t, :], ACT.Sigmoid), (qT[:, t, :], ACT.Silu), (v_tok[:, t, :], ACT.Gelu),
                           (i_tok[:, t, :], ACT.Copy), (y_sb[:, t, 0:HALF], ACT.Silu),
                           (y_sb[:, t, HALF:D], ACT.Gelu)][blk]
                if j == 4 * NT:
                    act.wait_ge(bn_done, 1)
                    act.activation(ln_r[:, :], bn2[:, :, 1], ACT.Sqrt).then_inc(ln_sd, 1)
                act.wait_ge(z_done, j + 1)
                act.activation(dst, bank[:, j % Z_BANKS, :], fn).then_inc(z_out, 1)
            for h in range(G):
                act.wait_ge(kt_done, h + 1)
                act.activation(k_tok[:, h].rearrange("p c k -> p (c k)"), bank[:, 5 + h % 2, :], ACT.Copy)\
                   .then_inc(kt_ready, 1)
            for h in range(G):
                act.wait_ge(o_done, h + 1)
                if h >= 2:
                    act.wait_ge(o_ms, h - 1)
                act.activation(squares[:, h % 2, :], bank[:, [2, 7, 3, 4][h], :], ACT.Square).then_inc(o_sq, 1)
            act.wait_ge(o_ms, G + 1)
            act.activation(o_r[:, :, :], o_ss[:, :, :], ACT.Sqrt).then_inc(o_sd, 1)

            def transposed_out(n):
                t = Y_GROUP.index(n) if n in Y_GROUP else H_GROUP.index(n)
                act.wait_ge(T_done, n + 1)
                act.activation(hT[:, 0:4, t * P:(t + 1) * P],
                               bank[:, 2 * (n % 2), :].rearrange("p (k t) -> p k t", k=4), ACT.Copy).then_inc(T_a, 1)

            def mean_square(t):
                act.wait_ge(x2_ready, 2 * t + 2)
                act.activation(junk[:, t, :], x_sb[:, t, :], ACT.Square, accum_out=stat_2[:, t, 0:1]).then_inc(x2_ss, 1)
                act.wait_ge(x2_ms, t + 1)
                act.activation(stat_2[:, t, 2:3], stat_2[:, t, 1:2], ACT.Sqrt).then_inc(x2_sd, 1)

            for n in range(3):
                transposed_out(n)
            mean_square(0)
            transposed_out(3)
            transposed_out(4)
            for t in range(1, NT):
                mean_square(t)
                transposed_out(t + 4)
            act.wait_ge(x2_ss, NT)
            act.dma_start(gain_fin, norm_final.unsqueeze(0).to_broadcast([P, D])).then_inc(fin_loaded, 16)
            act.wait_ge(r_dve, 1)
            act.activation(g_exp, g_exp, ACT.Exp).then_inc(r_act, 1)
            act.wait_ge(r_dve, 2)
            act.activation(egap, gap, ACT.Exp).then_inc(r_act, 1)

            act.wait_ge(steps_ready, 1)
            n_double = double_steps(act)

            def gathered_T(n):
                act.wait_ge(hgT_done, n)
                act.activation(hgT[:, 0:4, :], bank[:, 3, :].rearrange("p (k s) -> p k s", k=4), ACT.Copy)\
                   .then_inc(hgT_a, 1)

            def silu(n):
                act.wait_ge(gu_done, n)
                act.activation(silu_g, bank[:, 0, 0:F], ACT.Silu).then_inc(silu_done, 1)

            def hidden_T(n):
                act.wait_ge(hidT_done, n)
                act.activation(hidT, bank[:, 5, 0:F].rearrange("p (k s) -> p k s", k=KF), ACT.Copy)\
                   .then_inc(hidT_ready, 1)

            def rows_out(b, n, uses):
                act.wait_ge(down_done, n)
                if uses is not None:
                    act.wait_ge(scattered[b], uses)
                act.activation(yo[b][:, 0:HALF], bank[:, 1, :], ACT.Copy).then_inc(yo_a, 1)

            gathered_T(1)
            silu(1)
            gathered_T(2)
            hidden_T(1)
            silu(2)
            rows_out(0, 1, None)
            gathered_T(3)
            hidden_T(2)
            silu(3)
            rows_out(1, 2, None)
            gathered_T(4)
            hidden_T(3)
            with act.Fori(1, n_double - 1) as i:
                for b in (1, 0):
                    o = 1 if b else 2
                    silu(i * 2 + (o + 1))
                    rows_out(1 - b, i * 2 + o, i * 16)
                    gathered_T(i * 2 + (o + 2))
                    hidden_T(i * 2 + (o + 1))
            silu(n_double * 2)
            rows_out(0, n_double * 2 - 1, n_double * 16 - 16)
            hidden_T(n_double * 2)
            rows_out(1, n_double * 2, n_double * 16 - 16)

            for t in range(NT):
                act.wait_ge(f_y, t + 1)
                act.activation(junk_last[:, t, :], x_sb[:, t, :], ACT.Square, accum_out=stat_f[:, t, 0:1])\
                   .then_inc(f_ss, 1)
                act.wait_ge(f_ms, t + 1)
                act.activation(stat_f[:, t, 2:3], stat_f[:, t, 1:2], ACT.Sqrt).then_inc(f_sd, 1)

        @block.vector
        def _(dve):
            n_link = [0]

            def link(ins):
                n_link[0] += 1
                ins.then_inc(s_dve, 1)
                dve.wait_ge(s_dve, n_link[0])

            dve.memset(tab[:, :, :], EMPTY)
            dve.wait_ge(x_ss, NT)
            dve.tensor_scalar(stat_x[:, :, 1], stat_x[:, :, 0], 1.0 / D, RMS_EPS, ALU.mult, ALU.add).then_inc(x_ms, 1)
            dve.wait_ge(x_sd, 1)
            link(dve.reciprocal(stat_x[:, :, 3], stat_x[:, :, 2]))
            for t in range(NT):
                dve.tensor_scalar(y_sb[:, t, :], x_sb[:, t, :], stat_x[:, t, 3:4], None, ALU.mult)\
                   .then_inc(xn_ready, 1)
            dve.wait_ge(s_gain, 16)
            for k in range(1, KD, 2):
                dve.wait_ge(xT_done, k + 1)
                dve.tensor_scalar(hT[:, k, :], bank[:, 4, :], gain_mix[:, k:k + 1], None, ALU.mult)\
                   .then_inc(hT_odd, 1)
            for h in range(G):
                dve.wait_ge(z_out, h + 1)
                dve.tensor_scalar(kT[:, h, :], fT[:, h, :], -1.0, 1.0, ALU.mult, ALU.add)
                dve.tensor_scalar(fT[:, h, :], fT[:, h, :], F_FLOOR, None, ALU.max).then_inc(fk_ready, 1)

            def merge(n, h):
                j = 1 << (n - 1)
                f = fT[:, h, :].rearrange("p (b two j) -> p b two j", two=2, j=j)
                dve.wait_ge(decayed, n * G + h + 1)
                dve.tensor_tensor(f[:, :, 1, j - 1], f[:, :, 1, j - 1], f[:, :, 0, j - 1],
                                  ALU.mult).then_inc(f_merged, 1)

            def level(n):
                for h in range(G):
                    u = n * G + h
                    dve.wait_ge(attn_done, u + 1)
                    src = bank[:, 5 + h % 2, :].rearrange("p (c t) -> p c t", c=NT)
                    if n == 0:
                        dve.wait_ge(s_const, 5)
                        dve.tensor_tensor(attn[:, h], src, ident[:, :].unsqueeze(1).to_broadcast([P, NT, C]),
                                          ALU.mult).then_inc(attn_kept, 1)
                        dve.wait_ge(fk_ready, G)
                        dve.tensor_tensor(qT[:, h, :], qT[:, h, :], fT[:, h, :], ALU.mult).then_inc(decayed, 1)
                        continue
                    dve.wait_ge(attn_kept, u - G + 1)
                    dve.copy_predicated(attn[:, h], level_mask[:, n - 1, :].unsqueeze(1).to_broadcast([P, NT, C])
                                        .bitcast(I32), src).then_inc(attn_kept, 1)
                    j = 1 << (n - 1)
                    q, k, f = (a[:, h, :].rearrange("p (b two j) -> p b two j", two=2, j=j) for a in (qT, kT, fT))
                    nb = T // (2 * j)
                    if n >= 2:
                        dve.wait_ge(f_merged, (n - 2) * G + h + 1)
                    dve.wait_ge(decayed, (n - 1) * G + h + 1)
                    dve.tensor_tensor(q[:, :, 1, :], q[:, :, 1, :],
                                      f[:, :, 0, j - 1:j].to_broadcast([P, nb, j]), ALU.mult)
                    dve.tensor_tensor(k[:, :, 0, :], k[:, :, 0, :],
                                      f[:, :, 1, j - 1:j].to_broadcast([P, nb, j]), ALU.mult).then_inc(decayed, 1)
                    if h >= 1:
                        merge(n, h - 1)
                if n >= 1:
                    merge(n, G - 1)

            level(0)
            level(1)
            for t in range(NT):
                dve.wait_ge(z_out, 2 * NT + t + 1)
                for g in range(G):
                    last = dve.bn_stats(bn6[:, t, g, :], v_tok[:, t, g * C:(g + 1) * C])
                link(last)
                for g in range(G):
                    last = dve.bn_aggr(bn2[:, t * G + g, :], bn6[:, t, g, :])
            link(last)
            dve.tensor_scalar(bn2[:, :, 1], bn2[:, :, 1], LN_EPS, None, ALU.add).then_inc(bn_done, 1)
            for n in range(2, 6):
                level(n)
            dve.wait_ge(ln_sd, 1)
            link(dve.reciprocal(ln_r[:, :], ln_r[:, :]))
            for t in range(NT):
                for g in range(G):
                    n = t * G + g
                    last = dve.tensor_scalar(v_tok[:, t, g * C:(g + 1) * C], v_tok[:, t, g * C:(g + 1) * C],
                                             bn2[:, n, 0:1], ln_r[:, n:n + 1], ALU.subtract, ALU.mult)
                last.then_inc(ln_norm, 1)
            level(6)
            level(7)
            for g in range(G):
                dve.wait_ge(mixed_done, g + 1)
                dve.wait_ge(z_out, NZ)
                dve.wait_ge(wsT_ready, 1)
                u = y_sb[:, :, HALF + g * C:HALF + (g + 1) * C]
                dve.scalar_tensor_tensor(out=u, in0=bank[:, 3 + g % 2, :].rearrange("p (n c) -> p n c", n=NT),
                                         scalar=bsT[:, g:g + 1], in1=u, op0=ALU.add, op1=ALU.mult)\
                   .then_inc(u_ready, 1)
            dve.wait_ge(f_merged, LEVELS * G)
            for h in range(G):
                dve.wait_ge(upd_done, h + 1)
                ub = bank[:, h % 2, :].rearrange("p (c v) -> p c v", c=NT)
                link(dve.tensor_copy(states[:, h, 0, :], ub[:, 0, :]))
                for c in range(1, NT - 1):
                    ins = dve.scalar_tensor_tensor(out=states[:, h, c, :], in0=states[:, h, c - 1, :],
                                                   scalar=fT[:, h, (c + 1) * C - 1:(c + 1) * C],
                                                   in1=ub[:, c, :], op0=ALU.mult, op1=ALU.add)
                    if c < NT - 2:
                        link(ins)
                    else:
                        ins.then_inc(state_ready, 1)
            for h in range(G):
                dve.wait_ge(o_sq, h + 1)
                dve.reduce_sum(o_ss[:, h, :], squares[:, h % 2, :].rearrange("p (c v) -> p c v", c=NT), axis=AX)\
                   .then_inc(o_ms, 1)
            dve.wait_ge(o_ms, G)
            dve.tensor_scalar(o_ss[:, :, :], o_ss[:, :, :], 1.0 / C, RMS_EPS, ALU.mult, ALU.add).then_inc(o_ms, 1)
            dve.wait_ge(o_sd, 1)
            link(dve.reciprocal(o_r[:, :, :], o_r[:, :, :]))
            dve.wait_ge(gg_ready, NT)
            for c in range(NT):
                for h in range(G):
                    gt = y_sb[:, c, h * C:(h + 1) * C]
                    last = dve.scalar_tensor_tensor(out=gt, in0=bank[:, [2, 7, 3, 4][h], c * C:(c + 1) * C],
                                                    scalar=o_r[:, h, c:c + 1], in1=gt, op0=ALU.mult, op1=ALU.mult)
                last.then_inc(y_ready, 1)

            def transposed_out(n):
                t = Y_GROUP.index(n) if n in Y_GROUP else H_GROUP.index(n)
                dve.wait_ge(T_done, n + 1)
                dve.tensor_copy(hT[:, 4:8, t * P:(t + 1) * P],
                                bank[:, 2 * (n % 2) + 1, :].rearrange("p (k t) -> p k t", k=4)).then_inc(T_d, 1)

            def residual_norm(t):
                for hf in range(2):
                    u = 2 * t + hf
                    dve.wait_ge(wo_done, u + 1)
                    dve.tensor_tensor(x_sb[:, t, hf * HALF:(hf + 1) * HALF], x_sb[:, t, hf * HALF:(hf + 1) * HALF],
                                      bank[:, 5 + u % 3, :], ALU.add).then_inc(x2_ready, 1)
                dve.wait_ge(x2_ss, t + 1)
                dve.tensor_scalar(stat_2[:, t, 1:2], stat_2[:, t, 0:1], 1.0 / D, RMS_EPS, ALU.mult, ALU.add)\
                   .then_inc(x2_ms, 1)
                dve.wait_ge(x2_sd, t + 1)
                link(dve.reciprocal(stat_2[:, t, 3:4], stat_2[:, t, 2:3]))
                dve.scalar_tensor_tensor(out=h2[:, t, :], in0=x_sb[:, t, :], scalar=stat_2[:, t, 3:4],
                                         in1=gain_ffn[:, :], op0=ALU.mult, op1=ALU.mult).then_inc(h2_ready, 1)

            for n in range(3):
                transposed_out(n)
            residual_norm(0)
            transposed_out(3)
            transposed_out(4)
            for t in range(1, NT):
                residual_norm(t)
                transposed_out(t + 4)

            dve.wait_ge(logit_done, NT)
            link(dve.tensor_copy(logits, bank[:, 4, 0:NT * NL].rearrange("p (t e) -> p t e", t=NT)))
            lg, le = logits[:, :, 0:NG], logits[:, :, NG:NL]
            link(dve.reduce_max(g_max[:, :, 0], lg, axis=AX))
            dve.tensor_tensor(g_exp, lg, g_max.to_broadcast([P, NT, NG]), ALU.subtract).then_inc(r_dve, 1)
            link(dve.tensor_tensor(g_hot, lg, g_max.to_broadcast([P, NT, NG]), ALU.is_equal))
            link(dve.tensor_tensor(g_pick, g_hot, first_w[:, :].unsqueeze(1).to_broadcast([P, NT, NG]), ALU.mult))
            link(dve.reduce_max(g_max[:, :, 0], g_pick, axis=AX))
            link(dve.tensor_tensor(g_hot, g_pick, g_max.to_broadcast([P, NT, NG]), ALU.is_equal))
            link(dve.memset(e_log, LOWEST))
            for t in range(NT):
                last = dve.copy_predicated(
                    e_log[:, t].rearrange("p (g e) -> p g e", g=NG),
                    g_hot[:, t].unsqueeze(2).to_broadcast([P, NG, EPG]).bitcast(I32),
                    le[:, t].rearrange("p (g e) -> p g e", g=NG))
            link(last)
            for t in range(NT):
                last = dve.max(top8[:, t], e_log[:, t])
            link(last)
            for t in range(NT):
                last = dve.max_index(idx8[:, t].bitcast(U32), top8[:, t], e_log[:, t])
            link(last)
            dve.tensor_tensor(gap, top8[:, :, 1], top8[:, :, 0], ALU.subtract).then_inc(r_dve, 1)
            link(dve.tensor_copy(top_i, idx8[:, :, 0:2].bitcast(U32)))
            hot_v = hot.rearrange("p t j e -> p (t j) e")
            link(dve.tensor_tensor(hot_v, iota_e[:, :].unsqueeze(1).to_broadcast([P, NT * 2, NE]),
                                   top_i.rearrange("p t j -> p (t j)").unsqueeze(2)
                                   .to_broadcast([P, NT * 2, NE]), ALU.is_equal))
            dve.tensor_tensor(hot_b[:, :, :], hot[:, :, 0, :], hot[:, :, 1, :], ALU.add).then_inc(rank_ops, 1)
            for kind in range(2):
                for parity in range(2):
                    last = dve.tensor_tensor(
                        deal[:, :, parity, kind, :], hot_v.rearrange("p n (q r) -> p n q r", r=2)[:, :, :, parity],
                        row_f[:, kind].rearrange("p t j -> p (t j)").unsqueeze(2)
                        .to_broadcast([P, NT * 2, PAIRS]), ALU.mult)
            last.then_inc(deal_ready, 1)
            dve.wait_ge(r_act, 1)
            link(dve.reduce_sum(g_sum, g_exp, axis=AX))
            dve.wait_ge(r_act, 2)
            link(dve.tensor_scalar(den, egap, 1.0, None, ALU.add))
            link(dve.tensor_tensor(den, den, g_sum, ALU.mult))
            link(dve.reciprocal(w_top[:, 0, :], den))
            dve.tensor_tensor(w_top[:, 1, :], w_top[:, 0, :], egap, ALU.mult)
            dve.wait_ge(rank_done, 1)
            rk = bank[:, 5, 0:NT * NE].rearrange("p (t e) -> p t e", t=NT)
            for j in range(2):
                last = dve.tensor_tensor(rank_all[:, :, j, :], hot[:, :, j, :], rk, ALU.mult)
            link(last)
            link(dve.reduce_sum(rank, rank_all.rearrange("p t j e -> p (t j) e"), axis=AX))

            def slots_of(c):
                dve.tensor_scalar(round_rank, rank, float(-c * SLOTS), None, ALU.add).then_inc(s_dve, 1)
                n_link[0] += 1
                dve.wait_ge(s_dve, n_link[0])
                dve.tensor_tensor(in_round[:, c % 2, :, :],
                                  iota_s[:, :].unsqueeze(1).to_broadcast([P, NT * 2, SLOTS]),
                                  round_rank.unsqueeze(2).to_broadcast([P, NT * 2, SLOTS]), ALU.is_equal)\
                   .then_inc(round_ready, 1)

            def later_slots_of(c):
                dve.tensor_scalar(round_rank, rank, float(-c * SLOTS), None, ALU.add).then_inc(later_step, 1)
                dve.wait_ge(later_step, c)
                dve.tensor_tensor(in_round[:, c % 2, :, :],
                                  iota_s[:, :].unsqueeze(1).to_broadcast([P, NT * 2, SLOTS]),
                                  round_rank.unsqueeze(2).to_broadcast([P, NT * 2, SLOTS]), ALU.is_equal)\
                   .then_inc(round_ready, 1)

            def table_of(c):
                dve.wait_ge(slots_done, c + 1)
                dve.tensor_scalar(tab[:, :, c * PAIRS:(c + 1) * PAIRS],
                                  bank[:, 6 + c % 2, 0:2 * PAIRS].rearrange("p (k q) -> p k q", k=2),
                                  float(EMPTY), None, ALU.add).then_inc(tab_ready, 1)

            slots_of(0)
            link(dve.reduce_max(most, bank[:, 5, NT * NE:(NT + 1) * NE], axis=AX))
            link(dve.tensor_scalar(over, limits[:, :], most, None, ALU.is_lt))
            link(dve.reduce_sum(most, over, axis=AX))
            dve.tensor_scalar(steps[:, :], most, float(PAIRS // 2), float(PAIRS // 2), ALU.mult,
                              ALU.subtract).then_inc(steps_ready, 1)
            table_of(0)
            dve.wait_ge(steps_ready, 1)
            extra = more_steps(dve)
            with dve.If(extra > 0):
                for c in range(1, ROUNDS):
                    later_slots_of(c)
                    table_of(c)

            n_double = extra + PAIRS // 2

            def gathered_T(n):
                dve.wait_ge(hgT_done, n)
                dve.tensor_copy(hgT[:, 4:8, :], bank[:, 4, :].rearrange("p (k s) -> p k s", k=4)).then_inc(hgT_d, 1)

            def hidden(n):
                dve.wait_ge(silu_done, n)
                dve.tensor_tensor(hid, silu_g, bank[:, 0, F:2 * F], ALU.mult).then_inc(hid_ready, 1)

            def rows_out(b, n, uses):
                dve.wait_ge(down_done, n)
                if uses is not None:
                    dve.wait_ge(scattered[b], uses)
                dve.tensor_copy(yo[b][:, HALF:D], bank[:, 2, :]).then_inc(yo_d, 1)

            gathered_T(1)
            hidden(1)
            gathered_T(2)
            hidden(2)
            rows_out(0, 1, None)
            gathered_T(3)
            hidden(3)
            rows_out(1, 2, None)
            gathered_T(4)
            with dve.Fori(1, n_double - 1) as i:
                for b in (1, 0):
                    o = 1 if b else 2
                    hidden(i * 2 + (o + 1))
                    rows_out(1 - b, i * 2 + o, i * 16)
                    gathered_T(i * 2 + (o + 2))
            hidden(n_double * 2)
            rows_out(0, n_double * 2 - 1, n_double * 16 - 16)
            rows_out(1, n_double * 2, n_double * 16 - 16)

            def combine(t):
                dve.wait_ge(er_loaded[t], 16)
                link(dve.scalar_tensor_tensor(out=x_sb[:, t, :], in0=er[t][:, 0, :], scalar=w_top[:, 0, t:t + 1],
                                              in1=x_sb[:, t, :], op0=ALU.mult, op1=ALU.add))
                dve.scalar_tensor_tensor(out=x_sb[:, t, :], in0=er[t][:, 1, :], scalar=w_top[:, 1, t:t + 1],
                                         in1=x_sb[:, t, :], op0=ALU.mult, op1=ALU.add).then_inc(f_y, 1)

            def last_norm(t):
                dve.wait_ge(f_ss, t + 1)
                dve.tensor_scalar(stat_f[:, t, 1:2], stat_f[:, t, 0:1], 1.0 / D, RMS_EPS, ALU.mult, ALU.add)\
                   .then_inc(f_ms, 1)
                dve.wait_ge(f_sd, t + 1)
                link(dve.reciprocal(stat_f[:, t, 3:4], stat_f[:, t, 2:3]))
                dve.scalar_tensor_tensor(out=y_sb[:, t, :], in0=x_sb[:, t, :], scalar=stat_f[:, t, 3:4],
                                         in1=gain_fin, op0=ALU.mult, op1=ALU.mult).then_inc(f_out, 1)

            dve.wait_ge(fin_loaded, 16)
            combine(0)
            for t in range(1, NT):
                combine(t)
                last_norm(t - 1)
            last_norm(NT - 1)

        @block.tensor
        def _(pe):
            def transposes(dst, src_of, n, done):
                for a in range(n):
                    last = pe.transpose(dst(a), src_of(a), ident[:, :])
                last.then_inc(done, 1)

            pe.wait_ge(s_const, 1)
            pe.wait_ge(xn_ready, NT)
            for k in range(KD):
                if k >= 2:
                    pe.wait_ge(hT_even if k % 2 == 0 else hT_odd, k // 2)
                transposes(lambda t: bank[:, 3 + k % 2, t * P:(t + 1) * P], lambda t: y_sb[:, t, k:D:KD], NT, xT_done)
            pe.wait_ge(s_const, 2)
            for g in range(G):
                pe.transpose(bank[:, 5, g * C:(g + 1) * C], ws_raw[:, g, :], ident[:, :])
            pe.transpose(bank[:, 6, 0:G], bs_raw[:, :], ident[0:G, 0:G]).then_inc(wsT_done, 1)

            def scores(n):
                for h in range(G):
                    u = n * G + h
                    if u < 2:
                        pe.wait_ge(wsT_ready, 1)
                    else:
                        pe.wait_ge(attn_kept, u - 1)
                    if n == 0:
                        pe.wait_ge(z_out, G + h + 1)
                        pe.wait_ge(fk_ready, h + 1)
                    else:
                        pe.wait_ge(decayed, u - G + 1)
                    for c in range(NT):
                        last = pe.matmul(bank[:, 5 + h % 2, c * C:(c + 1) * C], kT[:, h, c * C:(c + 1) * C],
                                         qT[:, h, c * C:(c + 1) * C], start=True, stop=True)
                    last.then_inc(attn_done, 1)

            pe.wait_ge(hT_even, KD // 2)
            pe.wait_ge(hT_odd, KD // 2)
            for j in range(NZ):
                blk, t = divmod(j, NT)
                wb = a_ring[:, blk % 2, :].rearrange("p (k n) -> p k n", k=KD)
                if t == 0:
                    pe.wait_ge(s_ring[blk % 2], 16 * (blk // 2 + 1))
                if j >= Z_BANKS:
                    pe.wait_ge(z_out, j - Z_BANKS + 1)
                for k in range(KD):
                    if blk < 2:
                        lhsT, rhs = wb[:, k, t * P:(t + 1) * P], hT[:, k, :]
                    else:
                        lhsT, rhs = hT[:, k, t * P:(t + 1) * P], wb[:, k, :]
                    last = pe.matmul(bank[:, j % Z_BANKS, :], lhsT, rhs, start=(k == 0), stop=(k == KD - 1))
                last.then_inc(z_done, 1)
                if j in LEVEL_AT:
                    scores(LEVEL_AT.index(j))
            pe.wait_ge(vn_ready, NT)
            for g in range(G):
                if g >= 2:
                    pe.wait_ge(u_ready, g - 1)
                pe.matmul(bank[:, 3 + g % 2, :].rearrange("p (n c) -> p n c", n=NT), wsT[:, g, :],
                          v_tok[:, :, g * C:(g + 1) * C], start=True, stop=True).then_inc(mixed_done, 1)
            for h in range(G):
                pe.wait_ge(decayed, LEVELS * G + h + 1)
                if h < 2:
                    pe.wait_ge(attn_kept, (LEVELS + 1) * G)
                else:
                    pe.wait_ge(kt_ready, h - 1)
                transposes(lambda c: bank[:, 5 + h % 2, c * C:(c + 1) * C], lambda c: kT[:, h, c * C:(c + 1) * C],
                           NT, kt_done)
            for h in range(G):
                pe.wait_ge(kt_ready, h + 1)
                pe.wait_ge(z_out, NZ)
                if h >= 2:
                    pe.wait_ge(state_ready, h - 1)
                for c in range(NT - 1):
                    last = pe.matmul(bank[:, h % 2, c * C:(c + 1) * C], k_tok[:, h, c, :],
                                     i_tok[:, c, h * C:(h + 1) * C], start=True, stop=True)
                last.then_inc(upd_done, 1)
            for h in range(G):
                ob = [2, 7, 3, 4][h]
                pe.wait_ge(u_ready, G)
                pe.wait_ge(state_ready, h + 1)
                for c in range(NT):
                    last = pe.matmul(bank[:, ob, c * C:(c + 1) * C], attn[:, h, c, :],
                                     i_tok[:, c, h * C:(h + 1) * C], start=True, stop=(c == 0))
                    if c:
                        last = pe.matmul(bank[:, ob, c * C:(c + 1) * C], qT[:, h, c * C:(c + 1) * C],
                                         states[:, h, c - 1, :], start=False, stop=True)
                last.then_inc(o_done, 1)

            groups = [0]

            def width_first(src, t):
                n = groups[0]
                if n >= 2:
                    pe.wait_ge(T_a, n - 1)
                    pe.wait_ge(T_d, n - 1)
                transposes(lambda k: bank[:, 2 * (n % 2) + k // 4, (k % 4) * P:(k % 4 + 1) * P],
                           lambda k: src[:, t, k:D:KD], KD, T_done)
                groups[0] += 1

            def project(t):
                pe.wait_ge(T_a, Y_GROUP[t] + 1)
                pe.wait_ge(T_d, Y_GROUP[t] + 1)
                for hf in range(2):
                    u = 2 * t + hf
                    if u >= 3:
                        pe.wait_ge(x2_ready, u - 2)
                    wb = a_ring[:, hf, :].rearrange("p (k n) -> p k n", k=KD)
                    for k in range(KD):
                        last = pe.matmul(bank[:, 5 + u % 3, :], hT[:, k, t * P:(t + 1) * P], wb[:, k, :],
                                         start=(k == 0), stop=(k == KD - 1))
                    last.then_inc(wo_done, 1)

            def h2_T(t):
                pe.wait_ge(h2_ready, t + 1)
                width_first(h2, t)

            def route(t):
                pe.wait_ge(T_a, H_GROUP[t] + 1)
                pe.wait_ge(T_d, H_GROUP[t] + 1)
                for k in range(KD):
                    last = pe.matmul(bank[:, 4, t * NL:(t + 1) * NL], hT[:, k, t * P:(t + 1) * P], wr[:, k, :],
                                     start=(k == 0), stop=(k == KD - 1))
                last.then_inc(logit_done, 1)

            pe.wait_ge(y_ready, NT)
            width_first(y_sb, 0)
            width_first(y_sb, 1)
            pe.wait_ge(s_ring[0], 16 * 4)
            pe.wait_ge(s_ring[1], 16 * 4)
            project(0)
            width_first(y_sb, 2)
            project(1)
            h2_T(0)
            width_first(y_sb, 3)
            project(2)
            route(0)
            h2_T(1)
            project(3)
            route(1)
            h2_T(2)
            route(2)
            h2_T(3)
            route(3)

            pe.wait_ge(rank_ops, 1)
            for t in range(NT + 1):
                cols = bank[:, 5, t * NE:(t + 1) * NE]
                for s in range(min(t + 1, NT)):
                    last = pe.matmul(cols, before_b[:, :] if s == t else ones_b[:, :], hot_b[:, s, :],
                                     start=(s == 0), stop=(s == min(t, NT - 1)))
            last.then_inc(rank_done, 1)
            pe.wait_ge(deal_ready, 1)

            def slot_rows(c):
                pe.wait_ge(round_ready, c + 1)
                if c >= 2:
                    pe.wait_ge(tab_ready, c - 1)
                for n in range(2 * NT):
                    for parity in range(2):
                        last = pe.matmul(bank[parity * SLOTS:(parity + 1) * SLOTS, 6 + c % 2, 0:2 * PAIRS],
                                         in_round[:, c % 2, n, :],
                                         deal[:, n, parity].rearrange("p k q -> p (k q)"),
                                         start=(n == 0), stop=(n == 2 * NT - 1))
                last.then_inc(slots_done, 1)

            slot_rows(0)
            pe.wait_ge(steps_ready, 1)
            extra = more_steps(pe)
            with pe.If(extra > 0):
                for c in range(1, ROUNDS):
                    slot_rows(c)

            n_double = extra + PAIRS // 2

            def gathered_T(b, uses):
                pe.wait_ge(gathered[b], uses)
                transposes(lambda k: bank[:, 3 + k // 4, (k % 4) * P:(k % 4 + 1) * P],
                           lambda k: hg[b][:, k:D:KD], KD, hgT_done)

            def gate_up(b, n, uses):
                pe.wait_ge(hgT_a, n)
                pe.wait_ge(hgT_d, n)
                pe.wait_ge(wgu_loaded[b], uses * 2)
                for k in range(KD):
                    for e in range(2):
                        w = wgu[b][:, e].rearrange("p g (k f) -> p g k f", k=KD)
                        last = pe.matmul(
                            bank[e * SLOTS:(e + 1) * SLOTS, 0, :].rearrange("p (g f) -> p g f", g=2),
                            hgT[:, k, e * SLOTS:(e + 1) * SLOTS], w[:, :, k, :],
                            start=(k == 0), stop=(k == KD - 1))
                last.then_inc(gu_done, 1)

            def hidden_T(n):
                pe.wait_ge(hid_ready, n)
                transposes(lambda k: bank[:, 5, k * P:(k + 1) * P], lambda k: hid[:, k:F:KF], KF, hidT_done)

            def down(b, n, uses, prev):
                pe.wait_ge(hidT_ready, n)
                if prev is not None:
                    pe.wait_ge(yo_a, prev)
                    pe.wait_ge(yo_d, prev)
                pe.wait_ge(wd_loaded[b], uses)
                for hf in range(2):
                    for k in range(KF):
                        for e in range(2):
                            w = wd[b][:, e].rearrange("p (k d) -> p k d", k=KF)
                            last = pe.matmul(bank[e * SLOTS:(e + 1) * SLOTS, 1 + hf, :],
                                             hidT[:, k, e * SLOTS:(e + 1) * SLOTS],
                                             w[:, k, hf * HALF:(hf + 1) * HALF],
                                             start=(k == 0), stop=(k == KF - 1))
                last.then_inc(down_done, 1)

            gathered_T(0, 16)
            gate_up(0, 1, 16)
            gathered_T(1, 16)
            hidden_T(1)
            gate_up(1, 2, 16)
            down(0, 1, 16, None)
            gathered_T(0, 32)
            hidden_T(2)
            gate_up(0, 3, 32)
            down(1, 2, 16, 1)
            gathered_T(1, 32)
            hidden_T(3)
            with pe.Fori(1, n_double - 1) as i:
                gate_up(1, i * 2 + 2, i * 16 + 16)
                down(0, i * 2 + 1, i * 16 + 16, i * 2)
                gathered_T(0, i * 16 + 32)
                hidden_T(i * 2 + 2)
                gate_up(0, i * 2 + 3, i * 16 + 32)
                down(1, i * 2 + 2, i * 16 + 16, i * 2 + 1)
                gathered_T(1, i * 16 + 32)
                hidden_T(i * 2 + 3)
            gate_up(1, n_double * 2, n_double * 16)
            down(0, n_double * 2 - 1, n_double * 16, n_double * 2 - 2)
            hidden_T(n_double * 2)
            down(1, n_double * 2, n_double * 16, n_double * 2 - 1)


_INS = ["x", "norm_mix", "w_in", "hgrn_norm", "tmlp_ln_g", "tmlp_ln_b", "w_spatial", "b_spatial", "w_out",
        "norm_ffn", "w_router_group", "w_router_expert", "w_gate", "w_up", "w_down", "norm_final"]


def kernel(**inputs):
    import numpy as np
    import concourse.bacc as bacc
    from concourse.bass_utils import run_bass_kernel_spmd

    nc = bacc.Bacc("TRN2", target_bir_lowering=False, num_devices=1)
    arrays, args = {}, []
    for name in _INS:
        a = np.ascontiguousarray(inputs[name])
        if name != "norm_final":
            a = a.reshape(a.shape[1:])
        arrays[name + "_in"] = a
        args.append(nc.dram_tensor(name + "_in", a.shape, F32, kind="ExternalInput").ap())
    out = nc.dram_tensor("out", arrays["x_in"].shape, F32, kind="ExternalOutput").ap()
    hybrid_trunk(nc, *args, out)
    r = run_bass_kernel_spmd(nc, [arrays], core_ids=[0])
    return r.results[0]["out"].reshape(np.shape(inputs["x"]))
```

```python
from contextlib import ExitStack

import concourse.bass as bass
from concourse import mybir

ALU = mybir.AluOpType
ACT = mybir.ActivationFunctionType
AX = mybir.AxisListType.X
F32 = mybir.dt.float32
F32R = mybir.dt.float32r
BF16 = mybir.dt.bfloat16
I32 = mybir.dt.int32
U32 = mybir.dt.uint32

P = 128
RMS_EPS = 1e-6
LN_EPS = 1e-5
F_FLOOR = 1e-30
SLOTS = 64
EMPTY = 4096
LOWEST = -3.0e38


def hybrid_trunk(nc, x, norm_mix, w_in, hgrn_norm, ln_g, ln_b, w_spatial, b_spatial, w_out,
                 norm_ffn, w_rg, w_re, w_gate, w_up, w_down, norm_final, out):
    T, D = x.shape
    NT, KD = T // P, D // P
    G = w_spatial.shape[0]
    C = w_spatial.shape[1]
    NG = w_rg.shape[1]
    NE = w_re.shape[1]
    EPG = NE // NG
    F = w_gate.shape[2]
    KF = F // P
    NL = NG + NE
    HALF = D // 2
    UNIT = 2 * P
    PAIRS = NE // 2
    ROUNDS = T // SLOTS
    LEVELS = C.bit_length() - 1
    assert G * C == HALF and C == P and F == 2 * P and NT == 4 and SLOTS * 2 == P
    assert w_in.shape[1] == 6 * HALF and PAIRS % 2 == 0

    expert_rows = nc.dram_tensor("expert_rows", (2 * T, D), F32, kind="Internal").ap()

    w_in_v = w_in.rearrange("(p k) e -> p k e", k=KD)
    w_out_v = w_out.rearrange("(p k) e -> p k e", k=KD)

    with ExitStack() as ctx:
        def sb(name, shape, dt=F32):
            return ctx.enter_context(nc.sbuf_tensor(name, shape, dt))

        def sem(name):
            return ctx.enter_context(nc.semaphore(name))

        x_sb = sb("x_sb", [P, NT, D])
        arena = sb("arena", [P, KD * T + 4 * KD * HALF + 3 * NT * D + G * T + 2 * HALF])
        arena_at = nc.lookup_mloc(arena).addr

        def at(name, first, shape, dt=F32):
            return nc.alloc_sbuf_tensor_at(name, shape, dt, offset=arena_at + 4 * first)

        R0, R1, R2, R3 = 0, KD * T, KD * T + 2 * KD * HALF, KD * T + 4 * KD * HALF
        hi_T = at("hi_T", R0, [P, KD, T], F32R)
        a_hT = at("a_hT", R0, [P, KD * T])
        w_raw = at("w_raw", R1, [P, 2, KD, UNIT])
        lo_T = at("lo_T", R1 + 2 * KD * UNIT, [P, KD, T], F32R)
        wgu1 = at("wgu1", R1, [P, 2, 2, KD * F])
        w_hi = at("w_hi", R2, [P, 2, KD, UNIT], F32R)
        w_lo = at("w_lo", R2 + 2 * KD * UNIT, [P, 2, KD, UNIT], F32R)
        wgu0 = at("wgu0", R2, [P, 2, 2, KD * F])
        a_fk = sb("a_fk", [P, 2, G, T])
        fT, kT = a_fk[:, 0], a_fk[:, 1]
        R4 = R3 + 3 * NT * D
        R5 = R4 + G * T
        a_iv = at("a_iv", R3, [P, 2, NT, HALF])
        y_sb = at("y_sb", R3 + NT * D, [P, NT, D])
        a_ak = at("a_ak", R3 + 2 * NT * D, [P, 2, G, NT, C])
        h2_part = [at("h2_part0", R4, [P, NT, D], BF16), at("h2_part1", R3, [P, NT, D], BF16),
                   at("h2_part2", R3 + NT * D // 2, [P, NT, D], BF16)]
        wgu_spare = at("wgu_spare", R3 + NT * D, [P, 2, 2, KD * F])
        out_sb = at("out_sb", R3, [P, NT, D])
        er_sb = at("er_sb", R3 + NT * D, [P, NT, 2, D])
        qT = at("qT", R4, [P, G, T])
        lng = at("lng", R5, [P, HALF])
        lnb = at("lnb", R5 + HALF, [P, HALF])
        fills = at("fills", R5, [P, NT * 2, P], BF16)
        slot_of = at("slot_of", R5 + HALF, [P, 2, NT, P], BF16)
        wd0 = sb("wd0", [P, 2, KF * D])

        hT = a_hT[:, :].rearrange("p (k t) -> p k t", k=KD)
        states = a_fk[:, 1].rearrange("p h t -> p (h t)")[:, 0:G * (NT - 1) * C]\
            .rearrange("p (h c v) -> p h c v", h=G, c=NT - 1)
        squares = a_fk[:, 0, 0:2, :]
        junk = a_ak[:, :, :, :, :].rearrange("p a h c v -> p (a h c v)").rearrange("p (t d) -> p t d", t=NT)
        junk_last = wgu1[:, 0].rearrange("p g n -> p (g n)").rearrange("p (t d) -> p t d", t=NT)
        i_tok, v_tok = a_iv[:, 0], a_iv[:, 1]
        h2 = y_sb
        attn, k_tok = a_ak[:, 0], a_ak[:, 1]
        wgu = [wgu0[:, :, :, :], wgu1[:, :, :, :], wgu_spare[:, :, :, :]]
        wd = [wd0[:, :, :], a_hT[:, :].rearrange("p (e n) -> p e n", e=2)]
        SPARE = 2
        fT_flat = fT.rearrange("p h t -> p (h t)")
        hgT = fT_flat[:, 0:KD * P].rearrange("p (k s) -> p k s", k=KD)
        silu_g = fT_flat[:, KD * P:KD * P + F]
        hid = fT_flat[:, KD * P + F:KD * P + 2 * F]
        hidT = fT_flat[:, KD * P + 2 * F:KD * P + 3 * F].rearrange("p (k s) -> p k s", k=KF)
        yo = [kT.rearrange("p h t -> p (h t)")[:, b * D:(b + 1) * D] for b in range(2)]
        er = [er_sb[:, t] for t in range(NT)]

        ident = sb("ident", [P, P])
        ones_b = sb("ones_b", [P, P], BF16)
        before_b = sb("before_b", [P, P], BF16)
        level_mask = sb("level_mask", [P, LEVELS, C])
        gain_mix = sb("gain_mix", [P, KD])
        gnorm = sb("gnorm", [P, C])
        ws_raw = sb("ws_raw", [P, G, C])
        wsT = sb("wsT", [P, G, C])
        bs_raw = sb("bs_raw", [G, C])
        bsT = sb("bsT", [P, G])
        gain_ffn = sb("gain_ffn", [P, D])
        wr_g = sb("wr_g", [P, KD, NG])
        wr_e = sb("wr_e", [P, KD, NE])
        wr = sb("wr", [P, KD, NL])
        stat_x, stat_2, stat_f = (sb(n, [P, NT, 4]) for n in ("stat_x", "stat_2", "stat_f"))
        bn6 = sb("bn6", [P, NT, G, 6])
        bn2 = sb("bn2", [P, NT * G, 2])
        ln_r = sb("ln_r", [P, NT * G])
        o_ss = sb("o_ss", [P, G, NT])
        o_r = sb("o_r", [P, G, NT])
        tab = sb("tab", [P, ROUNDS * PAIRS], I32)
        cur = sb("cur", [P, 2], I32)
        slot_no = sb("slot_no", [P, NT * 2])
        steps = sb("steps", [P, 1], I32)
        w_top = sb("w_top", [P, 2, NT])

        rt_flat = a_fk[:, :, :, :].rearrange("p a h t -> p (a h t)")
        rt_used = [0, G * T]

        def rt(half, *shape):
            n = 1
            for d in shape:
                n *= d
            v = rt_flat[:, rt_used[half]:rt_used[half] + n]
            rt_used[half] += n
            assert rt_used[half] <= (half + 1) * G * T
            if len(shape) == 2:
                return v.rearrange("p (a b) -> p a b", a=shape[0])
            if len(shape) == 3:
                return v.rearrange("p (a b c) -> p a b c", a=shape[0], b=shape[1])
            return v

        logits_T = rt(0, T)[0:NL, :]
        logits = rt(0, NT, NL)
        g_max = rt(0, NT, 1)
        g_pick = rt(0, NT, NG)
        g_hot = rt(0, NT, NG)
        e_log = rt(0, NT, NE)
        top8 = rt(0, NT, 8)
        idx8 = rt(0, NT, 8)
        rank_all = rt(0, NT, 2, NE)
        past = rt(0, NT * 2, ROUNDS - 1)
        round_of = rt(0, NT * 2)
        top_i = rt(1, NT, 2)
        g_exp = rt(1, NT, NG)
        g_sum = rt(1, NT)
        gap = rt(1, NT)
        egap = rt(1, NT)
        den = rt(1, NT)
        hot = rt(1, NT, 2, NE)
        rank = rt(1, NT * 2)
        round_rank = rt(1, NT * 2)
        deal = rt(1, NT * 2, 2, PAIRS)
        in_round = rt(1, 2, NT * 2, SLOTS)
        most = rt(1, 1)
        over = rt(1, ROUNDS)
        gain_fin = gain_ffn[:, :]
        hot_b = sb("hot_b", [P, NT, NE], BF16)
        iota_e = sb("iota_e", [P, NE])
        iota_s = sb("iota_s", [P, P])
        iota_i = sb("iota_i", [P, P], I32)
        row_i = sb("row_i", [P, NT, 2], I32)
        row_f = sb("row_f", [P, NT, 2])
        first_w = sb("first_w", [P, NG])
        limits = sb("limits", [P, ROUNDS])

        bank = ctx.enter_context(nc.psum_tensor("bank", [P, 8, HALF], F32))

        s_x = [sem(f"x_loaded{t}") for t in range(NT)]
        s_gain = sem("gain_mix_loaded")
        s_small = sem("small_loaded")
        raw_loaded = [sem(f"raw_loaded{b}") for b in range(2)]
        w_hi_ready = sem("w_hi_ready")
        w_lo_ready = sem("w_lo_ready")
        s_const = sem("const_made")
        s_cstep = sem("const_step")
        warm = sem("warm_value")
        x_ss = sem("x_ss")
        x_ms = sem("x_ms")
        x_sd = sem("x_sd")
        x_rs = sem("x_rs")
        xn_act = sem("xn_act")
        xn_ready = sem("xn_ready")
        xT_done = sem("xT_done")
        hT_hi = sem("hT_hi")
        hT_lo = sem("hT_lo")
        wsT_done = sem("wsT_done")
        wsT_ready = sem("wsT_ready")
        z_done = sem("z_done")
        z_out = sem("z_out")
        fk_ready = sem("fk_ready")
        attn_done = sem("attn_done")
        attn_kept = sem("attn_kept")
        decayed = sem("decayed")
        f_merged = sem("f_merged")
        bn_done = sem("bn_done")
        ln_sd = sem("ln_sd")
        ln_norm = sem("ln_norm")
        vn_ready = sem("vn_ready")
        gg_ready = sem("gg_ready")
        mixed_done = sem("mixed_done")
        kt_done = sem("ktok_done")
        kt_ready = sem("ktok_ready")
        upd_done = sem("update_done")
        state_ready = sem("state_ready")
        o_done = sem("o_done")
        o_sq = sem("o_sq")
        o_ms = sem("o_ms")
        o_sd = sem("o_sd")
        y_ready = sem("y_ready")
        yT_done = sem("yT_done")
        yT_hi = sem("yT_hi")
        yT_lo = sem("yT_lo")
        h2T_done = sem("h2T_done")
        h2T_a = sem("h2T_act")
        h2T_d = sem("h2T_dve")
        wo_done = sem("w_out_done")
        x2_ready = sem("x2_ready")
        x2_ss = sem("x2_ss")
        x2_ms = sem("x2_ms")
        x2_sd = sem("x2_sd")
        h2_ready = sem("h2_ready")
        part_ready = [sem(f"h2_part{n}_ready") for n in range(3)]
        rest_ready = sem("h2_rest_ready")
        logit_done = sem("logits_done")
        logits_T_ready = sem("logits_T_ready")
        logit_back = sem("logits_by_token")
        r_dve = sem("router_dve")
        r_act = sem("router_act")
        rank_ops = sem("rank_ops")
        rank_done = sem("rank_done")
        steps_ready = sem("steps_ready")
        deal_ready = sem("deal_ready")
        round_ready = sem("round_ready")
        slots_done = sem("slots_done")
        tab_ready = sem("tab_ready")
        later_step = sem("later_step")
        fills_ready = sem("fills_ready")
        slot_of_ready = sem("slot_of_ready")
        slot_no_moved = sem("slot_no_moved")
        wgu_loaded = [sem(f"wgu_loaded{b}") for b in range(3)]
        wd_loaded = [sem(f"wd_loaded{b}") for b in range(2)]
        cur_ready = sem("cur_ready")
        scattered = [sem(f"scattered{b}") for b in range(2)]
        hgT_done = sem("hgT_done")
        hgT_a = sem("hgT_act")
        hgT_d = sem("hgT_dve")
        gu_done = sem("gate_up_done")
        silu_done = sem("silu_done")
        hid_ready = sem("hid_ready")
        hidT_done = sem("hidT_done")
        hidT_ready = sem("hidT_ready")
        down_done = sem("down_done")
        yo_a = sem("yo_act")
        yo_d = sem("yo_dve")
        er_loaded = [sem(f"er_loaded{n}") for n in range(2 * NT)]
        fin_loaded = sem("gain_fin_loaded")
        f_dve = sem("final_dve")
        f_y = sem("final_y")
        f_ss = sem("final_ss")
        f_ms = sem("final_ms")
        f_sd = sem("final_sd")
        f_rs = sem("final_rs")
        f_scaled = sem("final_scaled")
        f_out = sem("final_out")
        f_last = sem("final_last")
        out_stored = sem("out_stored")
        s_dve = sem("dve_step")

        block = ctx.enter_context(nc.Block())

        SMALL = 8
        COL = [1, 0, 5, 2, 3, 4]
        UNITS_IN, UNITS = 12, 16
        NZ = 2 * NT + 8 * NT
        K_AT, UPDATE_AT, HEADS_AT = 33, 35, 37
        LOGIT_BANK = [4, 6, 5, 4]
        O_BANK, MIX_BANK = [7, 3, 4, 5], [6, 0, 1, 2]
        LEVEL_AT = [2 * NT + 1 + 3 * n for n in range(LEVELS + 1)]
        Z_BANKS = 3

        def more_steps(eng):
            return eng.value_load(steps[0:1, 0:1], min_val=0, max_val=(ROUNDS - 1) * PAIRS // 2)

        def double_steps(eng):
            return more_steps(eng) + PAIRS // 2

        def z_count(blk, t):
            return blk * NT + t + 1 if blk < 2 else 2 * NT + (blk - 2) * 2 * NT + NT + t + 1

        def unit_done(u):
            return 2 * (u + 1) if u < 4 else 2 * NT + (u - 3) * NT

        def pair_w(w, q):
            return w[q * 2:q * 2 + 2] if isinstance(q, int) else w[bass.ds(q * 2, 2)]

        def load_gate_up(sp, b, q):
            for g, w in enumerate((w_gate, w_up)):
                sp.dma_start(wgu[b][:, :, g, :],
                             pair_w(w, q).rearrange("e (p k) f -> p e (k f)", k=KD)).then_inc(wgu_loaded[b], 16)

        def load_down(sp, b, q):
            sp.dma_start(wd[b], pair_w(w_down, q).rearrange("e (p k) d -> p e (k d)", k=KF))\
              .then_inc(wd_loaded[b], 16)

        @block.sync
        def _(sp):
            for t in range(NT):
                sp.dma_start(x_sb[:, t, :], x[t * P:(t + 1) * P, :]).then_inc(s_x[t], 16)
            loads = [(ws_raw[:, :, :], w_spatial.rearrange("g t s -> t g s")),
                     (bs_raw[:, :], b_spatial),
                     (gnorm[:, :], hgrn_norm.unsqueeze(0).to_broadcast([P, C])),
                     (lng[:, :], ln_g.unsqueeze(0).to_broadcast([P, HALF])),
                     (lnb[:, :], ln_b.unsqueeze(0).to_broadcast([P, HALF])),
                     (gain_ffn[:, :], norm_ffn.unsqueeze(0).to_broadcast([P, D])),
                     (wr_g[:, :, :], w_rg.rearrange("(p k) e -> p k e", k=KD)),
                     (wr_e[:, :, :], w_re.rearrange("(p k) e -> p k e", k=KD))]
            assert len(loads) == SMALL
            for u in range(UNITS):
                if u < UNITS_IN:
                    c0 = COL[u // 2] * HALF + (u % 2) * UNIT
                    src = w_in_v[:, :, c0:c0 + UNIT]
                else:
                    src = w_out_v[:, :, (u - UNITS_IN) * UNIT:(u - UNITS_IN + 1) * UNIT]
                if u >= 2:
                    sp.wait_ge(w_lo_ready, u - 1)
                sp.dma_start(w_raw[:, u % 2], src).then_inc(raw_loaded[u % 2], 16)
                if u == 1:
                    for dst, small in loads:
                        sp.dma_start(dst, small).then_inc(s_small, 16)
                if u == 3:
                    load_down(sp, 0, 0)
            sp.wait_ge(wo_done, 4 * NT)
            load_gate_up(sp, 0, 0)
            load_gate_up(sp, 1, 1)
            sp.wait_ge(logit_done, NT)
            load_down(sp, 1, 1)
            sp.wait_ge(part_ready[2], NT)
            load_gate_up(sp, SPARE, 2)
            sp.wait_ge(steps_ready, 1)
            n_double = double_steps(sp)

            def next_gate_up(b, n, pair):
                sp.wait_ge(gu_done, n)
                load_gate_up(sp, b, pair)

            def next_down(b, n, pair):
                sp.wait_ge(down_done, n)
                load_down(sp, b, pair)

            next_gate_up(0, 1, 4)
            next_gate_up(1, 2, 3)
            next_down(0, 1, 2)
            next_down(1, 2, 3)
            next_gate_up(SPARE, 3, 5)
            next_down(0, 3, 4)
            next_gate_up(1, 4, 7)
            next_down(1, 4, 5)
            next_gate_up(0, 5, 6)
            next_down(0, 5, 6)
            next_down(1, 6, 7)
            with sp.Fori(4, n_double) as m:
                for b in range(2):
                    pair = (m % (PAIRS // 2)) * 2 + b
                    next_gate_up(b, m * 2 + (b - 1), pair)
                    next_down(b, m * 2 + (b - 1), pair)
            for b in range(2):
                sp.wait_ge(scattered[b], n_double * 16)
            for t in range(NT):
                rows = expert_rows[2 * t * P:2 * (t + 1) * P, :].rearrange("(p j) d -> p j d", j=2)
                for j in range(2):
                    sp.dma_start(er[t][:, j, :], rows[:, j, :]).then_inc(er_loaded[2 * t + j], 16)
            for t in range(NT):
                sp.wait_ge(f_out if t < 2 else f_last, t + 1 if t < 2 else t - 1)
                sp.dma_start(out[t * P:(t + 1) * P, :], out_sb[:, t, :]).then_inc(out_stored, 16)
            sp.wait_ge(out_stored, 16 * NT)

        @block.gpsimd
        def _(pool):
            made = [0]

            def step(ins):
                made[0] += 1
                ins.then_inc(s_cstep, 1)
                pool.wait_ge(s_cstep, made[0])

            step(pool.memset(ident[:, :], 0.0))
            pool.affine_select(out=ident[:, :], in_=ident[:, :], compare_op=ALU.not_equal, fill=1.0, base=0,
                               pattern=[[-1, P]], channel_multiplier=1).then_inc(s_const, 1)
            pool.wait_ge(w_hi_ready, 1)
            pool.tensor_tensor(w_lo[:, 0], w_raw[:, 0], w_hi[:, 0].bitcast(F32), ALU.subtract).then_inc(w_lo_ready, 1)
            pool.wait_ge(s_small, 16 * SMALL)
            pool.affine_select(out=ws_raw[:, :, :], in_=ws_raw[:, :, :], compare_op=ALU.is_ge, fill=0.0, base=0,
                               pattern=[[0, G], [-1, C]], channel_multiplier=1).then_inc(s_const, 1)
            step(pool.memset(level_mask[:, :, :], 0.0))
            for n in range(LEVELS):
                h = 1 << n
                right = level_mask[:, n, :].rearrange("p (b two j) -> p b two j", two=2, j=h)[:, :, 1, :]
                nb = C // (2 * h)
                step(pool.memset(right, 1.0))
                step(pool.affine_select(out=right, in_=right, compare_op=ALU.is_ge, fill=0.0, base=0,
                                        pattern=[[-2 * h, nb], [0, h]], channel_multiplier=1))
                last = pool.affine_select(out=right, in_=right, compare_op=ALU.is_ge, fill=0.0, base=h - 1,
                                          pattern=[[2 * h, nb], [0, h]], channel_multiplier=-1)
            last.then_inc(s_const, 1)
            step(pool.memset(ones_b[:, :], 1.0))
            pool.affine_select(out=before_b[:, :], in_=ones_b[:, :], compare_op=ALU.is_gt, fill=0.0, base=0,
                               pattern=[[1, P]], channel_multiplier=-1).then_inc(s_const, 1)
            step(pool.iota(iota_i[:, :], pattern=[[1, P]], base=0, channel_multiplier=0))
            pool.tensor_copy(iota_e[:, :], iota_i[:, 0:NE])
            pool.tensor_copy(iota_s[:, :], iota_i[:, :])
            step(pool.iota(row_i[:, :, :], pattern=[[2 * P, NT], [1, 2]], base=-EMPTY, channel_multiplier=2))
            pool.tensor_copy(row_f[:, :, :], row_i[:, :, :])
            pool.tensor_scalar(first_w[:, :], iota_i[:, 0:NG], -1.0, float(NG), ALU.mult, ALU.add)
            pool.tensor_scalar(limits[:, :], iota_i[:, 0:ROUNDS], float(SLOTS), 0.0, ALU.mult, ALU.add)
            pool.tensor_copy(wr[:, :, 0:NG], wr_g[:, :, :])
            pool.tensor_copy(wr[:, :, NG:NL], wr_e[:, :, :]).then_inc(s_const, 1)
            pool.wait_ge(ln_norm, NT)
            for t in range(NT):
                step(pool.tensor_tensor(v_tok[:, t, :], v_tok[:, t, :], lng[:, :], ALU.mult))
                pool.tensor_tensor(v_tok[:, t, :], v_tok[:, t, :], lnb[:, :], ALU.add).then_inc(vn_ready, 1)
            for t in range(NT):
                pool.wait_ge(z_out, z_count(4, t))
                gt = y_sb[:, t, 0:HALF].rearrange("p (h v) -> p h v", h=G)
                pool.tensor_tensor(gt, gt, gnorm[:, :].unsqueeze(1).to_broadcast([P, G, C]), ALU.mult)\
                    .then_inc(gg_ready, 1)
            for t in range(NT):
                pool.wait_ge(part_ready[0], t + 1)
                pool.wait_ge(h2T_done, t + 1)
                pool.tensor_tensor(h2[:, t, :], h2[:, t, :], h2_part[0][:, t, :], ALU.subtract)\
                    .then_inc(rest_ready, 1)
            for t in range(NT):
                pool.wait_ge(part_ready[1], t + 1)
                pool.wait_ge(rest_ready, t + 1)
                pool.tensor_tensor(h2_part[2][:, t, :], h2[:, t, :], h2_part[1][:, t, :], ALU.subtract)\
                    .then_inc(part_ready[2], 1)

            pool.wait_ge(steps_ready, 1)
            extra = more_steps(pool)
            n_double = extra + PAIRS // 2

            def scatter(b, step_n, limit):
                pool.wait_ge(yo_a, step_n + 1)
                pool.wait_ge(yo_d, step_n + 1)
                src = tab[:, step_n:step_n + 1] if isinstance(step_n, int) else tab[:, bass.ds(step_n, 1)]
                pool.tensor_copy(cur[:, b:b + 1], src).then_inc(cur_ready, 1)
                pool.wait_ge(cur_ready, step_n + 1)
                pool.indirect_dma_start(
                    expert_rows, bass.IndirectOffsetOnAxis(ap=cur[:, b:b + 1], axis=0), yo[b], None,
                    bounds_check=limit(), oob_is_err=False).then_inc(scattered[b], 16)

            pool.wait_ge(tab_ready, 1)
            scatter(0, 0, lambda: 2 * T - 1)
            with pool.If(extra > 0):
                pool.wait_ge(tab_ready, ROUNDS)
            with pool.Fori(1, n_double) as m:
                scatter(1, m * 2 - 1, lambda: pool.snap(m + (2 * T - 1)))
                scatter(0, m * 2, lambda: pool.snap(m + 2 * T))
            scatter(1, n_double * 2 - 1, lambda: pool.snap(n_double + (2 * T - 1)))
            pool.wait_ge(fin_loaded, 16)
            for t in range(2):
                pool.wait_ge(f_scaled, t + 1)
                pool.tensor_tensor(out_sb[:, t, :], out_sb[:, t, :], gain_fin, ALU.mult).then_inc(f_out, 1)

        @block.scalar
        def _(act):
            act.dma_start(gain_mix[:, :], norm_mix.rearrange("(p k) -> p k", k=KD)).then_inc(s_gain, 16)
            act.wait_ge(warm, 1)
            act.activation(stat_f[:, :, 0], stat_f[:, :, 1], ACT.Sqrt)
            for t in range(NT):
                act.wait_ge(s_x[t], 16)
                act.activation(junk[:, t, :], x_sb[:, t, :], ACT.Square, accum_out=stat_x[:, t, 0:1]).then_inc(x_ss, 1)
            act.wait_ge(x_ms, 1)
            act.activation(stat_x[:, :, 2], stat_x[:, :, 1], ACT.Sqrt).then_inc(x_sd, 1)
            def split_high(u):
                act.wait_ge(raw_loaded[u % 2], 16 * (u // 2 + 1))
                if u >= UNITS_IN + 2:
                    act.wait_ge(wo_done, NT * (u - UNITS_IN - 1))
                elif u >= 2:
                    act.wait_ge(z_done, unit_done(u - 2))
                act.activation(w_hi[:, u % 2], w_raw[:, u % 2], ACT.Copy).then_inc(w_hi_ready, 1)

            for t in range(2):
                act.wait_ge(x_rs, 1)
                act.activation(y_sb[:, t, :], x_sb[:, t, :], ACT.Copy, scale=stat_x[:, t, 3:4]).then_inc(xn_act, 1)
            split_high(0)
            act.wait_ge(s_gain, 16)
            for k in range(KD):
                act.wait_ge(xT_done, k + 1)
                act.activation(hi_T[:, k, :], bank[:, k, :], ACT.Copy, scale=gain_mix[:, k:k + 1])\
                   .then_inc(hT_hi, 1)
            def k_by_token():
                for h in range(G):
                    act.wait_ge(kt_done, h + 1)
                    act.activation(k_tok[:, h].rearrange("p c k -> p (c k)"), bank[:, 5 + h % 2, :], ACT.Copy)\
                       .then_inc(kt_ready, 1)

            def head_norms():
                for h in range(G):
                    act.wait_ge(o_done, h + 1)
                    if h >= 2:
                        act.wait_ge(o_ms, h - 1)
                    act.activation(squares[:, h % 2, :], bank[:, O_BANK[h], :], ACT.Square).then_inc(o_sq, 1)
                act.wait_ge(o_ms, G + 1)
                act.activation(o_r[:, :, :], o_ss[:, :, :], ACT.Sqrt).then_inc(o_sd, 1)

            split_high(1)
            for u in range(UNITS_IN):
                blk = u // 2
                if u >= 1:
                    split_high(u + 1)
                if blk == 4 and u % 2 == 0:
                    act.wait_ge(bn_done, 1)
                    act.activation(ln_r[:, :], bn2[:, :, 1], ACT.Sqrt).then_inc(ln_sd, 1)
                for n in range(2 if blk < 2 else NT):
                    j = unit_done(u - 1) + n
                    act.wait_ge(z_done, j + 1)
                    if blk < 2:
                        act.activation((fT, qT)[blk][:, j % NT, :], bank[:, j % Z_BANKS, :],
                                       (ACT.Sigmoid, ACT.Silu)[blk]).then_inc(z_out, 1)
                        if j == 1:
                            act.wait_ge(wsT_done, 1)
                            act.activation(wsT[:, :, :].rearrange("p g t -> p (g t)"), bank[:, 5, :], ACT.Copy)
                            act.activation(bsT[:, :], bank[:, 6, 0:G], ACT.Copy).then_inc(wsT_ready, 1)
                    else:
                        c0 = (u % 2) * UNIT
                        dst = [v_tok[:, n, c0:c0 + UNIT], i_tok[:, n, c0:c0 + UNIT], y_sb[:, n, c0:c0 + UNIT],
                               y_sb[:, n, HALF + c0:HALF + c0 + UNIT]][blk - 2]
                        act.activation(dst, bank[:, j % Z_BANKS, 0:UNIT],
                                       (ACT.Gelu, ACT.Copy, ACT.Silu, ACT.Gelu)[blk - 2]).then_inc(z_out, 1)
                    if j == K_AT:
                        k_by_token()
                    if j == HEADS_AT:
                        head_norms()
            split_high(UNITS_IN + 1)
            for t in range(NT):
                act.wait_ge(yT_done, t + 1)
                act.activation(hi_T[:, :, t * P:(t + 1) * P],
                               bank[:, 2 * (t % 2):2 * (t % 2) + 2, :].rearrange("p a (k t) -> p (a k) t", t=P),
                               ACT.Copy).then_inc(yT_hi, 1)
            split_high(UNITS_IN + 2)
            split_high(UNITS_IN + 3)

            def mean_square(t):
                act.wait_ge(x2_ready, 3 * NT + t + 1)
                act.activation(junk[:, t, :], x_sb[:, t, :], ACT.Square, accum_out=stat_2[:, t, 0:1]).then_inc(x2_ss, 1)
                act.wait_ge(x2_ms, t + 1)
                act.activation(stat_2[:, t, 2:3], stat_2[:, t, 1:2], ACT.Sqrt).then_inc(x2_sd, 1)

            def h2T_out(t):
                act.wait_ge(h2T_done, t + 1)
                act.activation(hT[:, 0:4, t * P:(t + 1) * P],
                               bank[:, 2 * (t % 2), :].rearrange("p (k t) -> p k t", k=4), ACT.Copy).then_inc(h2T_a, 1)

            def part(n, t):
                act.wait_ge(rest_ready if n else h2_ready, t + 1)
                act.activation(h2_part[n][:, t, :], h2[:, t, :], ACT.Copy).then_inc(part_ready[n], 1)

            def logits_T_out(t):
                act.wait_ge(logit_done, t + 1)
                act.activation(logits_T[:, t * P:(t + 1) * P], bank[0:NL, LOGIT_BANK[t], 0:P], ACT.Copy)\
                   .then_inc(logits_T_ready, 1)

            act.activation(stat_x[:, :, 2], stat_x[:, :, 1], ACT.Sqrt)
            mean_square(0)
            mean_square(1)
            part(0, 0)
            mean_square(2)
            h2T_out(0)
            mean_square(3)
            h2T_out(1)
            part(0, 1)
            h2T_out(2)
            part(0, 2)
            h2T_out(3)
            part(0, 3)
            logits_T_out(0)
            logits_T_out(1)
            part(1, 0)
            logits_T_out(2)
            logits_T_out(3)
            for t in range(1, NT):
                part(1, t)
            act.wait_ge(h2_ready, NT)
            act.dma_start(gain_fin, norm_final.unsqueeze(0).to_broadcast([P, D])).then_inc(fin_loaded, 16)
            act.wait_ge(r_dve, 1)
            act.activation(g_exp, g_exp, ACT.Exp).then_inc(r_act, 1)
            act.wait_ge(r_dve, 2)
            act.activation(egap, gap, ACT.Exp).then_inc(r_act, 1)

            act.wait_ge(steps_ready, 1)
            n_double = double_steps(act)

            def gathered_T(n):
                act.wait_ge(hgT_done, n)
                act.activation(hgT[:, 0:4, :], bank[:, 3, :].rearrange("p (k s) -> p k s", k=4), ACT.Copy)\
                   .then_inc(hgT_a, 1)

            def silu(n):
                act.wait_ge(gu_done, n)
                act.activation(silu_g, bank[:, 0, 0:F], ACT.Silu).then_inc(silu_done, 1)

            def hidden_T(n):
                act.wait_ge(hidT_done, n)
                act.activation(hidT, bank[:, 5, 0:F].rearrange("p (k s) -> p k s", k=KF), ACT.Copy)\
                   .then_inc(hidT_ready, 1)

            def rows_out(b, n, uses):
                act.wait_ge(down_done, n)
                if uses is not None:
                    act.wait_ge(scattered[b], uses)
                act.activation(yo[b][:, 0:HALF], bank[:, 1, :], ACT.Copy).then_inc(yo_a, 1)

            gathered_T(1)
            silu(1)
            gathered_T(2)
            hidden_T(1)
            silu(2)
            rows_out(0, 1, None)
            gathered_T(3)
            hidden_T(2)
            silu(3)
            rows_out(1, 2, None)
            gathered_T(4)
            hidden_T(3)
            with act.Fori(1, n_double - 1) as i:
                for b in (1, 0):
                    o = 1 if b else 2
                    silu(i * 2 + (o + 1))
                    rows_out(1 - b, i * 2 + o, i * 16)
                    gathered_T(i * 2 + (o + 2))
                    hidden_T(i * 2 + (o + 1))
            silu(n_double * 2)
            rows_out(0, n_double * 2 - 1, n_double * 16 - 16)
            hidden_T(n_double * 2)
            rows_out(1, n_double * 2, n_double * 16 - 16)

            def scale(t):
                act.wait_ge(f_rs, t + 1)
                act.activation(out_sb[:, t, :], x_sb[:, t, :], ACT.Copy, scale=stat_f[:, t, 3:4]).then_inc(f_scaled, 1)

            for t in range(NT):
                act.wait_ge(f_y, t + 1)
                act.activation(junk_last[:, t, :], x_sb[:, t, :], ACT.Square, accum_out=stat_f[:, t, 0:1])\
                   .then_inc(f_ss, 1)
                act.wait_ge(f_ms, t + 1)
                act.activation(stat_f[:, t, 2:3], stat_f[:, t, 1:2], ACT.Sqrt).then_inc(f_sd, 1)
                if t < 2:
                    scale(t)

        @block.vector
        def _(dve):
            n_link = [0]

            def link(ins):
                n_link[0] += 1
                ins.then_inc(s_dve, 1)
                dve.wait_ge(s_dve, n_link[0])

            dve.memset(stat_f[:, :, 1], 1.0).then_inc(warm, 1)
            dve.memset(tab[:, :], EMPTY)
            dve.wait_ge(x_ss, NT)
            dve.tensor_scalar(stat_x[:, :, 1], stat_x[:, :, 0], 1.0 / D, RMS_EPS, ALU.mult, ALU.add).then_inc(x_ms, 1)
            dve.wait_ge(x_sd, 1)
            dve.reciprocal(stat_x[:, :, 3], stat_x[:, :, 2]).then_inc(x_rs, 1)
            dve.wait_ge(x_rs, 1)
            for t in range(2, NT):
                dve.tensor_scalar(y_sb[:, t, :], x_sb[:, t, :], stat_x[:, t, 3:4], None, ALU.mult)\
                   .then_inc(xn_ready, 1)

            def split_low(u):
                dve.wait_ge(w_hi_ready, u + 1)
                dve.tensor_tensor(w_lo[:, u % 2], w_raw[:, u % 2], w_hi[:, u % 2].bitcast(F32), ALU.subtract)\
                   .then_inc(w_lo_ready, 1)

            for k in range(KD):
                dve.wait_ge(hT_hi, k + 1)
                dve.scalar_tensor_tensor(out=lo_T[:, k, :], in0=bank[:, k, :], scalar=gain_mix[:, k:k + 1],
                                         in1=hi_T[:, k, :].bitcast(F32), op0=ALU.mult, op1=ALU.subtract)\
                   .then_inc(hT_lo, 1)
            dve.wait_ge(w_lo_ready, 1)
            split_low(1)
            for h in range(G):
                if h >= 2:
                    split_low(h)
                dve.wait_ge(z_out, h + 1)
                dve.tensor_scalar(kT[:, h, :], fT[:, h, :], -1.0, 1.0, ALU.mult, ALU.add)
                dve.tensor_scalar(fT[:, h, :], fT[:, h, :], F_FLOOR, None, ALU.max).then_inc(fk_ready, 1)

            def merge(n, h):
                j = 1 << (n - 1)
                f = fT[:, h, :].rearrange("p (b two j) -> p b two j", two=2, j=j)
                dve.wait_ge(decayed, n * G + h + 1)
                dve.tensor_tensor(f[:, :, 1, j - 1], f[:, :, 1, j - 1], f[:, :, 0, j - 1],
                                  ALU.mult).then_inc(f_merged, 1)

            def level(n):
                for h in range(G):
                    u = n * G + h
                    dve.wait_ge(attn_done, u + 1)
                    src = bank[:, 5 + h % 2, :].rearrange("p (c t) -> p c t", c=NT)
                    if n == 0:
                        dve.wait_ge(s_const, 5)
                        dve.tensor_tensor(attn[:, h], src, ident[:, :].unsqueeze(1).to_broadcast([P, NT, C]),
                                          ALU.mult).then_inc(attn_kept, 1)
                        dve.wait_ge(fk_ready, G)
                        dve.tensor_tensor(qT[:, h, :], qT[:, h, :], fT[:, h, :], ALU.mult).then_inc(decayed, 1)
                        continue
                    dve.wait_ge(attn_kept, u - G + 1)
                    j = 1 << (n - 1)
                    mask = level_mask[:, n - 1, :].rearrange("p (b two j) -> p b two j", two=2, j=j)[:, :, 1, :]
                    dve.copy_predicated(
                        attn[:, h].rearrange("p c (b two j) -> p c b two j", two=2, j=j)[:, :, :, 1, :],
                        mask.unsqueeze(1).to_broadcast([P, NT, C // (2 * j), j]).bitcast(I32),
                        bank[:, 5 + h % 2, 0:T // 2].rearrange("p (c b j) -> p c b j", c=NT, j=j))\
                       .then_inc(attn_kept, 1)
                    q, k, f = (a[:, h, :].rearrange("p (b two j) -> p b two j", two=2, j=j) for a in (qT, kT, fT))
                    nb = T // (2 * j)
                    if n >= 2:
                        dve.wait_ge(f_merged, (n - 2) * G + h + 1)
                    dve.wait_ge(decayed, (n - 1) * G + h + 1)
                    dve.tensor_tensor(q[:, :, 1, :], q[:, :, 1, :],
                                      f[:, :, 0, j - 1:j].to_broadcast([P, nb, j]), ALU.mult)
                    dve.tensor_tensor(k[:, :, 0, :], k[:, :, 0, :],
                                      f[:, :, 1, j - 1:j].to_broadcast([P, nb, j]), ALU.mult).then_inc(decayed, 1)
                    if h >= 1:
                        merge(n, h - 1)
                if n >= 1:
                    merge(n, G - 1)

            split_low(4)
            split_low(5)
            level(0)
            level(1)
            split_low(6)
            for t in range(NT):
                dve.wait_ge(z_out, z_count(2, t))
                for g in range(G):
                    last = dve.bn_stats(bn6[:, t, g, :], v_tok[:, t, g * C:(g + 1) * C])
                link(last)
                for g in range(G):
                    last = dve.bn_aggr(bn2[:, t * G + g, :], bn6[:, t, g, :])
            link(last)
            dve.tensor_scalar(bn2[:, :, 1], bn2[:, :, 1], LN_EPS, None, ALU.add).then_inc(bn_done, 1)
            level(2)
            split_low(7)
            level(3)
            split_low(8)
            level(4)
            level(5)
            split_low(9)
            dve.wait_ge(ln_sd, 1)
            link(dve.reciprocal(ln_r[:, :], ln_r[:, :]))
            for t in range(NT):
                for g in range(G):
                    n = t * G + g
                    last = dve.tensor_scalar(v_tok[:, t, g * C:(g + 1) * C], v_tok[:, t, g * C:(g + 1) * C],
                                             bn2[:, n, 0:1], ln_r[:, n:n + 1], ALU.subtract, ALU.mult)
                last.then_inc(ln_norm, 1)
            level(6)
            split_low(10)
            level(7)
            split_low(11)
            dve.wait_ge(f_merged, LEVELS * G)
            for h in range(G):
                dve.wait_ge(upd_done, h + 1)
                ub = bank[:, 5 + h % 2, :].rearrange("p (c v) -> p c v", c=NT)
                link(dve.tensor_copy(states[:, h, 0, :], ub[:, 0, :]))
                for c in range(1, NT - 1):
                    ins = dve.scalar_tensor_tensor(out=states[:, h, c, :], in0=states[:, h, c - 1, :],
                                                   scalar=fT[:, h, (c + 1) * C - 1:(c + 1) * C],
                                                   in1=ub[:, c, :], op0=ALU.mult, op1=ALU.add)
                    if c < NT - 2:
                        link(ins)
                    else:
                        ins.then_inc(state_ready, 1)
            split_low(12)
            for h in range(G):
                dve.wait_ge(o_sq, h + 1)
                dve.reduce_sum(o_ss[:, h, :], squares[:, h % 2, :].rearrange("p (c v) -> p c v", c=NT), axis=AX)\
                   .then_inc(o_ms, 1)
            dve.wait_ge(o_ms, G)
            dve.tensor_scalar(o_ss[:, :, :], o_ss[:, :, :], 1.0 / C, RMS_EPS, ALU.mult, ALU.add).then_inc(o_ms, 1)
            dve.wait_ge(o_sd, 1)
            link(dve.reciprocal(o_r[:, :, :], o_r[:, :, :]))
            dve.wait_ge(gg_ready, NT)
            for c in range(NT):
                for h in range(G):
                    gt = y_sb[:, c, h * C:(h + 1) * C]
                    dve.scalar_tensor_tensor(out=gt, in0=bank[:, O_BANK[h], c * C:(c + 1) * C],
                                             scalar=o_r[:, h, c:c + 1], in1=gt, op0=ALU.mult, op1=ALU.mult)
            dve.wait_ge(z_out, NZ)
            dve.wait_ge(wsT_ready, 1)
            for g in range(G):
                dve.wait_ge(mixed_done, g + 1)
                u = y_sb[:, :, HALF + g * C:HALF + (g + 1) * C]
                dve.scalar_tensor_tensor(out=u, in0=bank[:, MIX_BANK[g], :].rearrange("p (n c) -> p n c", n=NT),
                                         scalar=bsT[:, g:g + 1], in1=u, op0=ALU.add, op1=ALU.mult)\
                   .then_inc(y_ready, 1)

            def residual(u, t):
                v = NT * u + t
                cols = x_sb[:, t, u * UNIT:(u + 1) * UNIT]
                dve.wait_ge(wo_done, v + 1)
                dve.tensor_tensor(cols, cols, bank[:, 5 + v % 3, 0:UNIT], ALU.add).then_inc(x2_ready, 1)

            for t in range(NT):
                if t == 2:
                    split_low(13)
                dve.wait_ge(yT_hi, t + 1)
                dve.tensor_tensor(lo_T[:, :, t * P:(t + 1) * P],
                                  bank[:, 2 * (t % 2):2 * (t % 2) + 2, :].rearrange("p a (k t) -> p (a k) t", t=P),
                                  hi_T[:, :, t * P:(t + 1) * P].bitcast(F32), ALU.subtract).then_inc(yT_lo, 1)
            for u in range(UNITS - UNITS_IN):
                if u >= 1 and u < 3:
                    split_low(UNITS_IN + 1 + u)
                for t in range(NT if u < 3 else 0):
                    residual(u, t)

            def norm_sum(t):
                dve.wait_ge(x2_ss, t + 1)
                dve.tensor_scalar(stat_2[:, t, 1:2], stat_2[:, t, 0:1], 1.0 / D, RMS_EPS, ALU.mult, ALU.add)\
                   .then_inc(x2_ms, 1)

            def norm_scale(t):
                dve.wait_ge(x2_sd, t + 1)
                link(dve.reciprocal(stat_2[:, t, 3:4], stat_2[:, t, 2:3]))
                dve.scalar_tensor_tensor(out=h2[:, t, :], in0=x_sb[:, t, :], scalar=stat_2[:, t, 3:4],
                                         in1=gain_ffn[:, :], op0=ALU.mult, op1=ALU.mult).then_inc(h2_ready, 1)

            def h2T_out(t):
                dve.wait_ge(h2T_done, t + 1)
                dve.tensor_copy(hT[:, 4:8, t * P:(t + 1) * P],
                                bank[:, 2 * (t % 2) + 1, :].rearrange("p (k t) -> p k t", k=4)).then_inc(h2T_d, 1)

            LAST = UNITS - UNITS_IN - 1
            residual(LAST, 0)
            norm_sum(0)
            norm_scale(0)
            residual(LAST, 1)
            norm_sum(1)
            residual(LAST, 2)
            norm_scale(1)
            norm_sum(2)
            residual(LAST, 3)
            norm_scale(2)
            h2T_out(0)
            norm_sum(3)
            norm_scale(3)
            for t in range(1, NT):
                h2T_out(t)

            link(dve.memset(e_log, LOWEST))
            dve.wait_ge(logit_back, NT)
            link(dve.tensor_copy(logits, bank[:, 7, 0:NT * NL].rearrange("p (t e) -> p t e", t=NT)))
            lg, le = logits[:, :, 0:NG], logits[:, :, NG:NL]
            link(dve.reduce_max(g_max[:, :, 0], lg, axis=AX))
            dve.tensor_tensor(g_exp, lg, g_max.to_broadcast([P, NT, NG]), ALU.subtract).then_inc(r_dve, 1)
            link(dve.tensor_tensor(g_hot, lg, g_max.to_broadcast([P, NT, NG]), ALU.is_equal))
            link(dve.tensor_tensor(g_pick, g_hot, first_w[:, :].unsqueeze(1).to_broadcast([P, NT, NG]), ALU.mult))
            link(dve.reduce_max(g_max[:, :, 0], g_pick, axis=AX))
            link(dve.tensor_tensor(g_hot, g_pick, g_max.to_broadcast([P, NT, NG]), ALU.is_equal))
            for t in range(NT):
                last = dve.copy_predicated(
                    e_log[:, t].rearrange("p (g e) -> p g e", g=NG),
                    g_hot[:, t].unsqueeze(2).to_broadcast([P, NG, EPG]).bitcast(I32),
                    le[:, t].rearrange("p (g e) -> p g e", g=NG))
            link(last)
            for t in range(NT):
                last = dve.max(top8[:, t], e_log[:, t])
            link(last)
            for t in range(NT):
                last = dve.max_index(idx8[:, t].bitcast(U32), top8[:, t], e_log[:, t])
            link(last)
            dve.tensor_tensor(gap, top8[:, :, 1], top8[:, :, 0], ALU.subtract).then_inc(r_dve, 1)
            link(dve.tensor_copy(top_i, idx8[:, :, 0:2].bitcast(U32)))
            hot_v = hot.rearrange("p t j e -> p (t j) e")
            link(dve.tensor_tensor(hot_v, iota_e[:, :].unsqueeze(1).to_broadcast([P, NT * 2, NE]),
                                   top_i.rearrange("p t j -> p (t j)").unsqueeze(2)
                                   .to_broadcast([P, NT * 2, NE]), ALU.is_equal))
            dve.tensor_tensor(hot_b[:, :, :], hot[:, :, 0, :], hot[:, :, 1, :], ALU.add).then_inc(rank_ops, 1)
            dve.wait_ge(rank_done, 1)
            rk = bank[:, 5, 0:NT * NE].rearrange("p (t e) -> p t e", t=NT)
            for j in range(2):
                last = dve.tensor_tensor(rank_all[:, :, j, :], hot[:, :, j, :], rk, ALU.mult)
            link(last)
            link(dve.reduce_sum(rank, rank_all.rearrange("p t j e -> p (t j) e"), axis=AX))

            link(dve.tensor_tensor(past, rank.unsqueeze(2).to_broadcast([P, NT * 2, ROUNDS - 1]),
                                   limits[:, 1:ROUNDS].unsqueeze(1).to_broadcast([P, NT * 2, ROUNDS - 1]),
                                   ALU.is_ge))
            link(dve.reduce_sum(round_of, past, axis=AX))
            link(dve.scalar_tensor_tensor(out=slot_no[:, :], in0=top_i.rearrange("p t j -> p (t j)"),
                                          scalar=float(SLOTS), in1=rank, op0=ALU.mult, op1=ALU.add))
            link(dve.scalar_tensor_tensor(out=slot_no[:, :], in0=round_of, scalar=float((NE - 1) * SLOTS),
                                          in1=slot_no[:, :], op0=ALU.mult, op1=ALU.add))
            def slots_of(c):
                dve.tensor_scalar(round_rank, rank, float(-c * SLOTS), None, ALU.add).then_inc(s_dve, 1)
                n_link[0] += 1
                dve.wait_ge(s_dve, n_link[0])
                dve.tensor_tensor(in_round[:, c % 2, :, :],
                                  iota_s[:, 0:SLOTS].unsqueeze(1).to_broadcast([P, NT * 2, SLOTS]),
                                  round_rank.unsqueeze(2).to_broadcast([P, NT * 2, SLOTS]), ALU.is_equal)\
                   .then_inc(round_ready, 1)

            def later_slots_of(c):
                dve.tensor_scalar(round_rank, rank, float(-c * SLOTS), None, ALU.add).then_inc(later_step, 1)
                dve.wait_ge(later_step, c)
                dve.tensor_tensor(in_round[:, c % 2, :, :],
                                  iota_s[:, 0:SLOTS].unsqueeze(1).to_broadcast([P, NT * 2, SLOTS]),
                                  round_rank.unsqueeze(2).to_broadcast([P, NT * 2, SLOTS]), ALU.is_equal)\
                   .then_inc(round_ready, 1)

            def table_of(c):
                dve.wait_ge(slots_done, c + 1)
                dve.tensor_scalar(tab[:, c * PAIRS:(c + 1) * PAIRS], bank[:, 6 + c % 2, 0:PAIRS],
                                  float(EMPTY), None, ALU.add).then_inc(tab_ready, 1)

            def place_tokens(n):
                dve.tensor_tensor(fills[:, :, :], iota_s[:, :].unsqueeze(1).to_broadcast([P, NT * 2, P]),
                                  slot_no[:, :].unsqueeze(2).to_broadcast([P, NT * 2, P]), ALU.is_equal)\
                   .then_inc(fills_ready, 1)
                dve.wait_ge(fills_ready, n)

            def merge_choices(b, n):
                by_choice = fills[:, :, :].rearrange("p (t j) s -> p t j s", j=2)
                dve.tensor_tensor(slot_of[:, b], by_choice[:, :, 0, :], by_choice[:, :, 1, :], ALU.add)\
                   .then_inc(slot_of_ready, 1)
                dve.tensor_scalar(slot_no[:, :], slot_no[:, :], float(-P), None, ALU.add).then_inc(slot_no_moved, 1)
                dve.wait_ge(slot_of_ready, n)
                dve.wait_ge(slot_no_moved, n)

            def slots_filled(b, n):
                place_tokens(n)
                merge_choices(b, n)

            def gathered_T(n):
                dve.wait_ge(hgT_done, n)
                dve.tensor_copy(hgT[:, 4:8, :], bank[:, 4, :].rearrange("p (k s) -> p k s", k=4)).then_inc(hgT_d, 1)

            slots_filled(0, 1)
            slots_of(0)
            for parity in range(2):
                last = dve.tensor_tensor(
                    deal[:, :, parity, :], hot_v.rearrange("p n (q r) -> p n q r", r=2)[:, :, :, parity],
                    row_f[:, :, :].rearrange("p t j -> p (t j)").unsqueeze(2)
                    .to_broadcast([P, NT * 2, PAIRS]), ALU.mult)
            last.then_inc(deal_ready, 1)
            link(dve.reduce_max(most, bank[:, 5, NT * NE:(NT + 1) * NE], axis=AX))
            link(dve.tensor_scalar(over, limits[:, :], most, None, ALU.is_lt))
            link(dve.reduce_sum(most, over, axis=AX))
            dve.tensor_scalar(steps[:, :], most, float(PAIRS // 2), float(PAIRS // 2), ALU.mult,
                              ALU.subtract).then_inc(steps_ready, 1)
            dve.wait_ge(r_act, 1)
            link(dve.reduce_sum(g_sum, g_exp, axis=AX))
            dve.wait_ge(r_act, 2)
            link(dve.tensor_scalar(den, egap, 1.0, None, ALU.add))
            link(dve.tensor_tensor(den, den, g_sum, ALU.mult))
            link(dve.reciprocal(w_top[:, 0, :], den))
            dve.tensor_tensor(w_top[:, 1, :], w_top[:, 0, :], egap, ALU.mult)
            slots_filled(1, 2)
            gathered_T(1)
            table_of(0)
            slots_filled(0, 3)
            dve.wait_ge(steps_ready, 1)
            extra = more_steps(dve)
            with dve.If(extra > 0):
                for c in range(1, ROUNDS):
                    later_slots_of(c)
                    table_of(c)

            n_double = extra + PAIRS // 2

            def hidden(n):
                dve.wait_ge(silu_done, n)
                dve.tensor_tensor(hid, silu_g, bank[:, 0, F:2 * F], ALU.mult).then_inc(hid_ready, 1)

            def rows_out(b, n, uses):
                dve.wait_ge(down_done, n)
                if uses is not None:
                    dve.wait_ge(scattered[b], uses)
                dve.tensor_copy(yo[b][:, HALF:D], bank[:, 2, :]).then_inc(yo_d, 1)

            hidden(1)
            gathered_T(2)
            slots_filled(1, 4)
            hidden(2)
            rows_out(0, 1, None)
            gathered_T(3)
            slots_filled(0, 5)
            hidden(3)
            rows_out(1, 2, None)
            gathered_T(4)
            slots_filled(1, 6)
            with dve.Fori(1, n_double - 1) as i:
                for b in (1, 0):
                    o = 1 if b else 2
                    hidden(i * 2 + (o + 1))
                    rows_out(1 - b, i * 2 + o, i * 16)
                    gathered_T(i * 2 + (o + 2))
                    slots_filled(1 - b, i * 2 + (o + 4))
            hidden(n_double * 2)
            rows_out(0, n_double * 2 - 1, n_double * 16 - 16)
            rows_out(1, n_double * 2, n_double * 16 - 16)

            def combine(t):
                dve.wait_ge(er_loaded[2 * t], 16)
                link(dve.scalar_tensor_tensor(out=x_sb[:, t, :], in0=er[t][:, 0, :], scalar=w_top[:, 0, t:t + 1],
                                              in1=x_sb[:, t, :], op0=ALU.mult, op1=ALU.add))
                dve.wait_ge(er_loaded[2 * t + 1], 16)
                dve.scalar_tensor_tensor(out=x_sb[:, t, :], in0=er[t][:, 1, :], scalar=w_top[:, 1, t:t + 1],
                                         in1=x_sb[:, t, :], op0=ALU.mult, op1=ALU.add).then_inc(f_y, 1)

            def last_norm(t):
                dve.wait_ge(f_ss, t + 1)
                dve.tensor_scalar(stat_f[:, t, 1:2], stat_f[:, t, 0:1], 1.0 / D, RMS_EPS, ALU.mult, ALU.add)\
                   .then_inc(f_ms, 1)
                dve.wait_ge(f_sd, t + 1)
                if t < 2:
                    dve.reciprocal(stat_f[:, t, 3:4], stat_f[:, t, 2:3]).then_inc(f_rs, 1)
                    return
                link(dve.reciprocal(stat_f[:, t, 3:4], stat_f[:, t, 2:3]))
                dve.scalar_tensor_tensor(out=out_sb[:, t, :], in0=x_sb[:, t, :], scalar=stat_f[:, t, 3:4],
                                         in1=gain_fin, op0=ALU.mult, op1=ALU.mult).then_inc(f_last, 1)

            dve.wait_ge(fin_loaded, 16)
            combine(0)
            for t in range(1, NT):
                combine(t)
                last_norm(t - 1)
            last_norm(NT - 1)

        @block.tensor
        def _(pe):
            def transposes(dst, src_of, n, done):
                for a in range(n):
                    last = pe.transpose(dst(a), src_of(a), ident[:, :])
                last.then_inc(done, 1)

            pe.wait_ge(s_const, 1)
            pe.wait_ge(xn_act, 2)
            pe.wait_ge(xn_ready, 2)
            for k in range(KD):
                transposes(lambda t: bank[:, k, t * P:(t + 1) * P], lambda t: y_sb[:, t, k:D:KD], NT, xT_done)
            def mixing_weights():
                pe.wait_ge(s_const, 2)
                for g in range(G):
                    pe.transpose(bank[:, 5, g * C:(g + 1) * C], ws_raw[:, g, :], ident[:, :])
                pe.transpose(bank[:, 6, 0:G], bs_raw[:, :], ident[0:G, 0:G]).then_inc(wsT_done, 1)

            def scores(n):
                for h in range(G):
                    u = n * G + h
                    if u < 2:
                        pe.wait_ge(wsT_ready, 1)
                    else:
                        pe.wait_ge(attn_kept, u - 1)
                    if n == 0:
                        pe.wait_ge(z_out, G + h + 1)
                        pe.wait_ge(fk_ready, h + 1)
                    else:
                        pe.wait_ge(decayed, u - G + 1)
                    for c in range(NT):
                        k_c, q_c = kT[:, h, c * C:(c + 1) * C], qT[:, h, c * C:(c + 1) * C]
                        if n == 0:
                            last = pe.matmul(bank[:, 5 + h % 2, c * C:(c + 1) * C], k_c, q_c, start=True, stop=True)
                        else:
                            j = 1 << (n - 1)
                            last = pe.matmul(bank[:, 5 + h % 2, c * C // 2:(c + 1) * C // 2]
                                             .rearrange("p (b j) -> p b j", j=j), k_c,
                                             q_c.rearrange("p (b two j) -> p b two j", two=2, j=j)[:, :, 1, :],
                                             start=True, stop=True)
                    last.then_inc(attn_done, 1)

            def product(dst, left, right):
                parts = [(0, 0), (0, 1), (1, 0)]
                for k in range(KD):
                    for n, (a, b) in enumerate(parts):
                        last = pe.matmul(dst, left[a](k), right[b](k), start=(k == 0 and n == 0),
                                         stop=(k == KD - 1 and n == 2))
                return last

            def tokens(t):
                return [lambda k: hi_T[:, k, t * P:(t + 1) * P], lambda k: lo_T[:, k, t * P:(t + 1) * P]]

            def unit(u):
                return [lambda k: w_hi[:, u % 2, k, :], lambda k: w_lo[:, u % 2, k, :]]

            def k_by_token():
                for h in range(G):
                    pe.wait_ge(decayed, LEVELS * G + h + 1)
                    if h < 2:
                        pe.wait_ge(attn_kept, (LEVELS + 1) * G)
                    else:
                        pe.wait_ge(kt_ready, h - 1)
                    transposes(lambda c: bank[:, 5 + h % 2, c * C:(c + 1) * C],
                               lambda c: kT[:, h, c * C:(c + 1) * C], NT, kt_done)

            def updates():
                pe.wait_ge(kt_ready, G)
                for h in range(G):
                    if h >= 2:
                        pe.wait_ge(state_ready, h - 1)
                    for c in range(NT - 1):
                        last = pe.matmul(bank[:, 5 + h % 2, c * C:(c + 1) * C], k_tok[:, h, c, :],
                                         i_tok[:, c, h * C:(h + 1) * C], start=True, stop=True)
                    last.then_inc(upd_done, 1)

            def heads():
                for h in range(G):
                    pe.wait_ge(state_ready, h + 1)
                    for c in range(NT):
                        cols = bank[:, O_BANK[h], c * C:(c + 1) * C]
                        last = pe.matmul(cols, attn[:, h, c, :], i_tok[:, c, h * C:(h + 1) * C],
                                         start=True, stop=(c == 0))
                        if c:
                            last = pe.matmul(cols, qT[:, h, c * C:(c + 1) * C], states[:, h, c - 1, :],
                                             start=False, stop=True)
                    last.then_inc(o_done, 1)

            def mix(g):
                pe.matmul(bank[:, MIX_BANK[g], :].rearrange("p (n c) -> p n c", n=NT), wsT[:, g, :],
                          v_tok[:, :, g * C:(g + 1) * C], start=True, stop=True).then_inc(mixed_done, 1)

            pe.wait_ge(hT_lo, KD)
            for u in range(UNITS_IN):
                pe.wait_ge(w_lo_ready, u + 1)
                for n in range(2 if u < 4 else NT):
                    j = unit_done(u - 1) + n
                    if j >= Z_BANKS:
                        pe.wait_ge(z_out, j - Z_BANKS + 1)
                    if u < 4:
                        cols = slice(n * P, (n + 1) * P)
                        last = product(bank[:, j % Z_BANKS, :],
                                       [lambda k: w_hi[:, u % 2, k, cols], lambda k: w_lo[:, u % 2, k, cols]],
                                       [lambda k: hi_T[:, k, :], lambda k: lo_T[:, k, :]])
                    else:
                        last = product(bank[:, j % Z_BANKS, 0:UNIT], tokens(n), unit(u))
                    last.then_inc(z_done, 1)
                    if j == 1:
                        mixing_weights()
                    if j in LEVEL_AT:
                        scores(LEVEL_AT.index(j))
                    if j == K_AT:
                        k_by_token()
                    if j == UPDATE_AT:
                        updates()
                    if j == HEADS_AT:
                        heads()
                        pe.wait_ge(vn_ready, NT)
                        mix(0)
            pe.wait_ge(z_out, NZ)
            for g in range(1, G):
                mix(g)

            def width_first(src, t, read_a, read_b, done):
                if t >= 2:
                    pe.wait_ge(read_a, t - 1)
                    pe.wait_ge(read_b, t - 1)
                transposes(lambda k: bank[:, 2 * (t % 2) + k // 4, (k % 4) * P:(k % 4 + 1) * P],
                           lambda k: src[:, t, k:D:KD], KD, done)

            def project(u, t):
                v = NT * u + t
                if v >= 3:
                    pe.wait_ge(x2_ready, v - 2)
                pe.wait_ge(yT_lo, t + 1)
                pe.wait_ge(w_lo_ready, UNITS_IN + u + 1)
                product(bank[:, 5 + v % 3, 0:UNIT], tokens(t), unit(u)).then_inc(wo_done, 1)

            def h2_T(t):
                pe.wait_ge(h2_ready, t + 1)
                width_first(h2, t, h2T_a, h2T_d, h2T_done)

            def route(t):
                pe.wait_ge(h2T_a, t + 1)
                pe.wait_ge(h2T_d, t + 1)
                if t == 3:
                    pe.wait_ge(logits_T_ready, 1)
                for k in range(KD):
                    last = pe.matmul(bank[0:NL, LOGIT_BANK[t], 0:P], wr[:, k, :], hT[:, k, t * P:(t + 1) * P],
                                     start=(k == 0), stop=(k == KD - 1))
                last.then_inc(logit_done, 1)

            def logits_by_token(t):
                pe.wait_ge(logits_T_ready, t + 1)
                pe.transpose(bank[:, 7, t * NL:(t + 1) * NL], logits_T[:, t * P:(t + 1) * P], ident[0:NL, 0:NL])\
                  .then_inc(logit_back, 1)

            pe.wait_ge(y_ready, G)
            width_first(y_sb, 0, yT_hi, yT_lo, yT_done)
            width_first(y_sb, 1, yT_hi, yT_lo, yT_done)
            project(0, 0)
            width_first(y_sb, 2, yT_hi, yT_lo, yT_done)
            project(0, 1)
            width_first(y_sb, 3, yT_hi, yT_lo, yT_done)
            project(0, 2)
            project(0, 3)
            for v in range(NT, NT * (UNITS - UNITS_IN) - 1):
                project(v // NT, v % NT)
            h2_T(0)
            project(UNITS - UNITS_IN - 1, NT - 1)
            h2_T(1)
            route(0)
            h2_T(2)
            route(1)
            h2_T(3)
            route(2)
            route(3)
            for t in range(NT):
                logits_by_token(t)

            pe.wait_ge(rank_ops, 1)
            for t in range(NT + 1):
                cols = bank[:, 5, t * NE:(t + 1) * NE]
                for s in range(min(t + 1, NT)):
                    last = pe.matmul(cols, before_b[:, :] if s == t else ones_b[:, :], hot_b[:, s, :],
                                     start=(s == 0), stop=(s == min(t, NT - 1)))
            last.then_inc(rank_done, 1)

            def slot_rows(c):
                pe.wait_ge(round_ready, c + 1)
                if c >= 2:
                    pe.wait_ge(tab_ready, c - 1)
                for n in range(2 * NT):
                    for parity in range(2):
                        last = pe.matmul(bank[parity * SLOTS:(parity + 1) * SLOTS, 6 + c % 2, 0:PAIRS],
                                         in_round[:, c % 2, n, :], deal[:, n, parity, :],
                                         start=(n == 0), stop=(n == 2 * NT - 1))
                last.then_inc(slots_done, 1)


            def gathered_T(b, n):
                pe.wait_ge(slot_of_ready, n)
                for k in range(KD):
                    for t in range(NT):
                        for p, part in enumerate(h2_part):
                            last = pe.matmul(bank[:, 3 + k // 4, (k % 4) * P:(k % 4 + 1) * P], part[:, t, k:D:KD],
                                             slot_of[:, b, t, :], start=(t == 0 and p == 0),
                                             stop=(t == NT - 1 and p == 2))
                last.then_inc(hgT_done, 1)

            def gate_up(b, n, uses):
                pe.wait_ge(hgT_a, n)
                pe.wait_ge(hgT_d, n)
                pe.wait_ge(wgu_loaded[b], uses * 2)
                for k in range(KD):
                    for e in range(2):
                        w = wgu[b][:, e].rearrange("p g (k f) -> p g k f", k=KD)
                        last = pe.matmul(
                            bank[e * SLOTS:(e + 1) * SLOTS, 0, :].rearrange("p (g f) -> p g f", g=2),
                            hgT[:, k, e * SLOTS:(e + 1) * SLOTS], w[:, :, k, :],
                            start=(k == 0), stop=(k == KD - 1))
                last.then_inc(gu_done, 1)

            def hidden_T(n):
                pe.wait_ge(hid_ready, n)
                transposes(lambda k: bank[:, 5, k * P:(k + 1) * P], lambda k: hid[:, k:F:KF], KF, hidT_done)

            def down(b, n, uses, prev):
                pe.wait_ge(hidT_ready, n)
                if prev is not None:
                    pe.wait_ge(yo_a, prev)
                    pe.wait_ge(yo_d, prev)
                pe.wait_ge(wd_loaded[b], uses)
                for hf in range(2):
                    for k in range(KF):
                        for e in range(2):
                            w = wd[b][:, e].rearrange("p (k d) -> p k d", k=KF)
                            last = pe.matmul(bank[e * SLOTS:(e + 1) * SLOTS, 1 + hf, :],
                                             hidT[:, k, e * SLOTS:(e + 1) * SLOTS],
                                             w[:, k, hf * HALF:(hf + 1) * HALF],
                                             start=(k == 0), stop=(k == KF - 1))
                last.then_inc(down_done, 1)

            pe.wait_ge(part_ready[2], NT)
            gathered_T(0, 1)
            pe.wait_ge(deal_ready, 1)
            slot_rows(0)
            gate_up(0, 1, 16)
            pe.wait_ge(steps_ready, 1)
            extra = more_steps(pe)
            with pe.If(extra > 0):
                for c in range(1, ROUNDS):
                    slot_rows(c)
            n_double = extra + PAIRS // 2
            gathered_T(1, 2)
            hidden_T(1)
            gate_up(1, 2, 16)
            down(0, 1, 16, None)
            gathered_T(0, 3)
            hidden_T(2)
            gate_up(SPARE, 3, 16)
            down(1, 2, 16, 1)
            gathered_T(1, 4)
            hidden_T(3)
            for i in range(1, 3):
                if i == 1:
                    gate_up(1, 4, 32)
                else:
                    gate_up(SPARE, 6, 32)
                down(0, i * 2 + 1, i * 16 + 16, i * 2)
                gathered_T(0, i * 2 + 3)
                hidden_T(i * 2 + 2)
                gate_up(0, i * 2 + 3, i * 16 + 16)
                down(1, i * 2 + 2, i * 16 + 16, i * 2 + 1)
                gathered_T(1, i * 2 + 4)
                hidden_T(i * 2 + 3)
            with pe.Fori(3, n_double - 1) as i:
                gate_up(1, i * 2 + 2, i * 16)
                down(0, i * 2 + 1, i * 16 + 16, i * 2)
                gathered_T(0, i * 2 + 3)
                hidden_T(i * 2 + 2)
                gate_up(0, i * 2 + 3, i * 16 + 16)
                down(1, i * 2 + 2, i * 16 + 16, i * 2 + 1)
                gathered_T(1, i * 2 + 4)
                hidden_T(i * 2 + 3)
            gate_up(1, n_double * 2, n_double * 16 - 16)
            down(0, n_double * 2 - 1, n_double * 16, n_double * 2 - 2)
            hidden_T(n_double * 2)
            down(1, n_double * 2, n_double * 16, n_double * 2 - 1)


_INS = ["x", "norm_mix", "w_in", "hgrn_norm", "tmlp_ln_g", "tmlp_ln_b", "w_spatial", "b_spatial", "w_out",
        "norm_ffn", "w_router_group", "w_router_expert", "w_gate", "w_up", "w_down", "norm_final"]


def kernel(**inputs):
    import numpy as np
    import concourse.bacc as bacc
    from concourse.bass_utils import run_bass_kernel_spmd

    nc = bacc.Bacc("TRN2", target_bir_lowering=False, num_devices=1)
    arrays, args = {}, []
    for name in _INS:
        a = np.ascontiguousarray(inputs[name])
        if name != "norm_final":
            a = a.reshape(a.shape[1:])
        arrays[name + "_in"] = a
        args.append(nc.dram_tensor(name + "_in", a.shape, F32, kind="ExternalInput").ap())
    out = nc.dram_tensor("out", arrays["x_in"].shape, F32, kind="ExternalOutput").ap()
    hybrid_trunk(nc, *args, out)
    r = run_bass_kernel_spmd(nc, [arrays], core_ids=[0])
    return r.results[0]["out"].reshape(np.shape(inputs["x"]))
```
